# Optimizing a Trainium2 kernel written in Bass

```python
import jax, jax.numpy as jnp
from jax import lax
import numpy as np

D_MODEL = 1024
BATCH = 1
SEQ = 2048
DEPTH = 1

CTX_LEN = 256
GRID_W = 64
N_HEADS = 8
HEAD_DIM = 64
ATT_W = N_HEADS * HEAD_DIM
CONV_W = 512
WIN_H_MAX = 8
WIN_W = 16
Q_COLS = 16
K_COLS = 32
D_FF = 2816
CONV_K = 3
EPS = 1e-6
NEG_INF = -1e30

Q_OFF = 0
K_OFF = ATT_W
V_OFF = 2 * ATT_W
BG_OFF = 3 * ATT_W
CG_OFF = BG_OFF + CONV_W
HV_OFF = CG_OFF + CONV_W
GA_OFF = HV_OFF + CONV_W
GB_OFF = GA_OFF + D_MODEL
IN_W = GB_OFF + D_MODEL

kernel_name = "hybrid_natten_shortconv_convffn_dit"

def rmsnorm(x, g):
    x32 = x.astype(jnp.float32)
    y = x32 * lax.rsqrt(jnp.mean(x32 * x32, axis=-1, keepdims=True) + EPS)
    return (y * g.astype(jnp.float32)).astype(x.dtype)

def modulate(h, shift, scale):
    return h * (1 + scale) + shift

def heads(t):
    return t.reshape(*t.shape[:-1], N_HEADS, HEAD_DIM)

def dwconv3(x, w):
    ch = x.shape[-1]
    return lax.conv_general_dilated(
        x, w[:, None, :].astype(x.dtype), window_strides=(1,), padding=((1, 1),),
        dimension_numbers=("NWC", "WIO", "NWC"), feature_group_count=ch)

def _col_blocks():
    n_cb = GRID_W // Q_COLS
    qcol = np.arange(GRID_W).reshape(n_cb, Q_COLS)
    cs = np.clip(qcol - WIN_W // 2, 0, GRID_W - WIN_W)
    kstart = np.clip(cs[:, 0], 0, GRID_W - K_COLS)
    kcol = kstart[:, None] + np.arange(K_COLS)
    valid = (kcol[:, None, :] >= cs[:, :, None]) & (kcol[:, None, :] < cs[:, :, None] + WIN_W)
    dc = np.clip(kcol[:, None, :] - qcol[:, :, None] + WIN_W - 1, 0, 2 * WIN_W - 2)
    return kcol, valid, dc

def neighbourhood_attention(q, k, v, kc, vc, rpb):
    b, s = q.shape[:2]
    rows = s // GRID_W
    kh = min(WIN_H_MAX, rows)
    n_cb = GRID_W // Q_COLS
    kcol, valid, dc = _col_blocks()
    mask = jnp.asarray(valid)[None, :, :, None, :]
    grid = lambda t: t.reshape(b, rows, GRID_W, N_HEADS, HEAD_DIM)
    qg = jnp.moveaxis(grid(q * (HEAD_DIM ** -0.5)), 1, 0)
    kg, vg = grid(k), grid(v)

    def one_row(args):
        r, q_row = args
        rs = jnp.clip(r - kh // 2, 0, rows - kh)
        k_rows = lax.dynamic_slice_in_dim(kg, rs, kh, axis=1)
        v_rows = lax.dynamic_slice_in_dim(vg, rs, kh, axis=1)
        kb = k_rows[:, :, kcol]
        vb = v_rows[:, :, kcol]
        qb = q_row.reshape(b, n_cb, Q_COLS, N_HEADS, HEAD_DIM)
        dr = rs + jnp.arange(kh) - r + WIN_H_MAX - 1
        bias = rpb[:, dr][:, :, dc]
        bias = jnp.where(mask, jnp.transpose(bias, (0, 2, 3, 1, 4)).astype(jnp.float32), NEG_INF)
        s_win = jnp.einsum("bnqhd,brnkhd->bhnqrk", qb, kb).astype(jnp.float32) + bias
        s_win = s_win.reshape(b, N_HEADS, n_cb, Q_COLS, kh * K_COLS)
        s_ctx = jnp.einsum("bnqhd,bjhd->bhnqj", qb, kc).astype(jnp.float32)
        p = jax.nn.softmax(jnp.concatenate([s_win, s_ctx], axis=-1), axis=-1)
        p_win = p[..., :kh * K_COLS].reshape(b, N_HEADS, n_cb, Q_COLS, kh, K_COLS).astype(v.dtype)
        p_ctx = p[..., kh * K_COLS:].astype(v.dtype)
        o = (jnp.einsum("bhnqrk,brnkhd->bnqhd", p_win, vb)
             + jnp.einsum("bhnqj,bjhd->bnqhd", p_ctx, vc))
        return o.reshape(b, GRID_W, N_HEADS, HEAD_DIM)

    out = lax.map(one_row, (jnp.arange(rows), qg))
    return jnp.moveaxis(out, 0, 1).reshape(b, s, ATT_W)

def context_attention(qc, kc, vc):
    b, n = qc.shape[:2]
    s = jnp.einsum("bihd,bjhd->bhij", qc * (HEAD_DIM ** -0.5), kc).astype(jnp.float32)
    p = jax.nn.softmax(s, axis=-1).astype(vc.dtype)
    return jnp.einsum("bhij,bjhd->bihd", p, vc).reshape(b, n, ATT_W)

def merge_branches(p, attn, w_conv, w_ba, w_bb, w_o):
    bg, cg, hv = p[..., BG_OFF:CG_OFF], p[..., CG_OFF:HV_OFF], p[..., HV_OFF:GA_OFF]
    ga, gb = p[..., GA_OFF:GB_OFF], p[..., GB_OFF:IN_W]
    y_attn = attn @ w_ba
    y_conv = (bg * dwconv3(cg * hv, w_conv)) @ w_bb
    return (jax.nn.sigmoid(ga) * y_attn + jax.nn.sigmoid(gb) * y_conv) @ w_o

def conv_ffn(h, w_up, w_conv, b_conv, w_down):
    u = h @ w_up
    a, g = u[..., :D_FF], u[..., D_FF:]
    return (jax.nn.gelu(dwconv3(g, w_conv) + b_conv, approximate=True) * a) @ w_down

def setup_inputs(seed: int = 0) -> dict:
    key = jax.random.key(seed)
    ks = jax.random.split(key, 20)
    n = jax.random.normal
    f32 = jnp.float32
    return {
        "x": n(ks[0], (BATCH, SEQ, D_MODEL), f32),
        "c": n(ks[1], (BATCH, D_MODEL), f32),
        "ctx": n(ks[2], (BATCH, CTX_LEN, D_MODEL), f32),
        "c_ctx": n(ks[3], (D_MODEL,), f32),
        "w_ada": n(ks[4], (DEPTH, D_MODEL, 6 * D_MODEL), f32) * (0.5 * D_MODEL ** -0.5),
        "b_ada": n(ks[5], (DEPTH, 6 * D_MODEL), f32) * 0.01,
        "g_pre_mix": 1.0 + 0.02 * n(ks[6], (DEPTH, D_MODEL), f32),
        "g_post_mix": 1.0 + 0.02 * n(ks[7], (DEPTH, D_MODEL), f32),
        "g_pre_ffn": 1.0 + 0.02 * n(ks[8], (DEPTH, D_MODEL), f32),
        "g_post_ffn": 1.0 + 0.02 * n(ks[9], (DEPTH, D_MODEL), f32),
        "w_in": n(ks[10], (DEPTH, D_MODEL, IN_W), f32) * D_MODEL ** -0.5,
        "rpb": n(ks[11], (DEPTH, N_HEADS, 2 * WIN_H_MAX - 1, 2 * WIN_W - 1), f32) * 0.1,
        "w_short_conv": n(ks[12], (DEPTH, CONV_K, CONV_W), f32) * CONV_K ** -0.5,
        "w_branch_attn": n(ks[13], (DEPTH, ATT_W, D_MODEL), f32) * ATT_W ** -0.5,
        "w_branch_conv": n(ks[14], (DEPTH, CONV_W, D_MODEL), f32) * CONV_W ** -0.5,
        "w_out": n(ks[15], (DEPTH, D_MODEL, D_MODEL), f32) * D_MODEL ** -0.5,
        "w_up": n(ks[16], (DEPTH, D_MODEL, 2 * D_FF), f32) * D_MODEL ** -0.5,
        "w_ffn_conv": n(ks[17], (DEPTH, CONV_K, D_FF), f32) * CONV_K ** -0.5,
        "b_ffn_conv": n(ks[18], (DEPTH, D_FF), f32) * 0.01,
        "w_down": n(ks[19], (DEPTH, D_FF, D_MODEL), f32) * D_FF ** -0.5,
    }

def reference(x, c, ctx, c_ctx, w_ada, b_ada, g_pre_mix, g_post_mix, g_pre_ffn, g_post_ffn,
              w_in, rpb, w_short_conv, w_branch_attn, w_branch_conv, w_out,
              w_up, w_ffn_conv, b_ffn_conv, w_down):
    for l in range(DEPTH):
        last = l == DEPTH - 1
        mod_x = (jax.nn.silu(c) @ w_ada[l] + b_ada[l])[:, None, :]
        mod_c = jax.nn.silu(c_ctx) @ w_ada[l] + b_ada[l]
        sh1, sc1, gt1, sh2, sc2, gt2 = jnp.split(mod_x, 6, axis=-1)
        csh1, csc1, cgt1, csh2, csc2, cgt2 = jnp.split(mod_c, 6, axis=-1)

        hc = modulate(rmsnorm(ctx, g_pre_mix[l]), csh1, csc1)
        if last:
            pkv = hc @ w_in[l][:, K_OFF:BG_OFF]
            kc, vc = heads(pkv[..., :ATT_W]), heads(pkv[..., ATT_W:])
        else:
            pc = hc @ w_in[l]
            kc, vc = heads(pc[..., K_OFF:V_OFF]), heads(pc[..., V_OFF:BG_OFF])
            attn_c = context_attention(heads(pc[..., Q_OFF:K_OFF]), kc, vc)
            yc = merge_branches(pc, attn_c, w_short_conv[l], w_branch_attn[l], w_branch_conv[l], w_out[l])
            ctx_mid = ctx + cgt1 * rmsnorm(yc, g_post_mix[l])
            hc2 = modulate(rmsnorm(ctx_mid, g_pre_ffn[l]), csh2, csc2)
            ctx = ctx_mid + cgt2 * rmsnorm(conv_ffn(hc2, w_up[l], w_ffn_conv[l], b_ffn_conv[l], w_down[l]), g_post_ffn[l])

        h = modulate(rmsnorm(x, g_pre_mix[l]), sh1, sc1)
        p = h @ w_in[l]
        attn = neighbourhood_attention(heads(p[..., Q_OFF:K_OFF]), heads(p[..., K_OFF:V_OFF]),
                                       heads(p[..., V_OFF:BG_OFF]), kc, vc, rpb[l])
        y = merge_branches(p, attn, w_short_conv[l], w_branch_attn[l], w_branch_conv[l], w_out[l])
        x = x + gt1 * rmsnorm(y, g_post_mix[l])

        h = modulate(rmsnorm(x, g_pre_ffn[l]), sh2, sc2)
        x = x + gt2 * rmsnorm(conv_ffn(h, w_up[l], w_ffn_conv[l], b_ffn_conv[l], w_down[l]), g_post_ffn[l])
    return x


_drawn_inputs = setup_inputs


def setup_inputs(seed=0):
    import zlib

    import numpy as np

    out = dict(_drawn_inputs(seed))
    spreads = {}
    factors = {'ctx': 2.854,
     'b_ada': 3.457,
     'g_pre_mix': 5.299,
     'g_post_mix': 8.0,
     'g_pre_ffn': 23.733,
     'g_post_ffn': 32.162,
     'rpb': 64.0,
     'b_ffn_conv': 62.508}
    for name, (base, spread) in spreads.items():
        noise = np.random.default_rng([zlib.crc32(name.encode()), seed]).standard_normal(out[name].shape)
        drawn = base * np.exp(spread * noise) if base else spread * noise
        out[name] = __import__('jax').numpy.asarray(drawn.astype(out[name].dtype))
    for name, factor in factors.items():
        out[name] = (out[name] * factor).astype(out[name].dtype)
    return out
```

```python
from contextlib import ExitStack, contextmanager

import numpy as np

import concourse.bass as bass
from concourse import mybir

ALU = mybir.AluOpType
ACT = mybir.ActivationFunctionType
AX = mybir.AxisListType
F32 = mybir.dt.float32
F32R = mybir.dt.float32r
I32 = mybir.dt.int32

P = 128
D = 1024
SEQ = 2048
CTX = 256
NTOK = SEQ + CTX
GRID_W = 64
HEADS = 8
DH = 64
ATT_W = HEADS * DH
CONV_W = 512
D_FF = 2816
WIN_H = 8
WIN_W = 16
EPS = 1e-6
NEG = -1e30
IN_W = 3 * ATT_W + 3 * CONV_W + 2 * D

KD = D // P
KA = ATT_W // P
BLK = 1024
NB = SEQ // BLK
HW = BLK + 2
HT = HW // 3
NT = 512
SC = 256
SLAB = KD * SC
RING = 3
FG = D_FF // SC
FC = D_FF // P
TT = SEQ // P
ROWS = SEQ // GRID_W
PAIRS = ROWS // 2
TROWS = 16
WROWS = 10
WIN = WROWS * GRID_W
TCOLS = TROWS * GRID_W + WIN


class Tally:

    def __init__(self, sem, credit):
        self.sem, self.credit = sem, credit
        self.seen = {}
        self.loops = {}

    def value(self, eng):
        i, per = self.loops.get(eng.engine, (None, 0))
        n = self.seen.get(eng.engine, 0) + self.credit
        return n if i is None else n + i * per

    def next(self, eng, k=1):
        self.seen[eng.engine] = self.seen.get(eng.engine, 0) + k
        return self.value(eng)

    def skip(self, eng, k):
        self.seen[eng.engine] = self.seen.get(eng.engine, 0) + k


class Signal:

    def __init__(self, env, name, credit=0):
        self.sem = env.stack.enter_context(env.nc.semaphore(name))
        self.credit = credit
        self.d = Tally(self.sem, credit)
        self.f = Tally(self.sem, 0)
        env.signals.append(self)
        if credit:
            env.credits.append(self)

    def drained(self, eng):
        return self.f.value(eng) + self.credit


@contextmanager
def repeat(eng, trips, per):
    e = eng.engine
    before = {t: t.seen.get(e, 0) for t in per}
    with eng.Fori(0, trips) as i:
        for t, n in per.items():
            t.loops[e] = (i, n)
        yield i
    for t, n in per.items():
        assert t.seen.get(e, 0) - before[t] == n, (t.sem, t.seen.get(e, 0) - before[t], n)
        t.seen[e] = before[t] + n * trips
        del t.loops[e]


class Env:
    pass


def slab(w, kc, col, cols):
    n = w.shape[-1]
    return bass.AP(tensor=w.tensor, offset=w.offset + col, ap=[[n, P], [P * n, kc], [1, cols]])


def product(pe, out, w, a, kc):
    for k in range(kc):
        w0, w1 = w(k)
        a0, a1 = a(k)
        pe.matmul(out, w0, a0, start=(k == 0), stop=False)
        pe.matmul(out, w0, a1, start=False, stop=False)
        last = pe.matmul(out, w1, a0, start=False, stop=(k == kc - 1))
    return last


def products_together(pe, tiles, kc, chunk_wait):
    for k in range(kc):
        chunk_wait(k)
        for out, w, a, done in tiles:
            w0, w1 = w(k)
            a0, a1 = a(k)
            pe.matmul(out, w0, a0, start=(k == 0), stop=False)
            pe.matmul(out, w0, a1, start=False, stop=False)
            last = pe.matmul(out, w1, a0, start=False, stop=(k == kc - 1))
            if k == kc - 1:
                last.then_inc(done.sem, 1)


def setup(nc, env, io):
    with ExitStack() as ctx:
        sb = lambda n, s, d=F32: ctx.enter_context(nc.sbuf_tensor(n, s, d))
        sig = lambda n: Signal(env, n)
        rows1 = sb("rows1", [108, P])
        rows2 = sb("rows2", [88, P])
        csig = sb("csig", [P, 16])
        csil = sb("csil", [P, 16])
        aw = sb("aw", [P, 4, SLAB])
        xr = sb("xr", [P, 3, D])
        sq = sb("sq", [P, D])
        xts = sb("xts", [P, 2, KD, NT])
        ss = sb("ss", [P, 18])
        rt = sb("rt", [P, 18])
        rr = sb("rr", [P, 18])
        rrow = sb("rrow", [18, P])
        modt = sb("modt", [P, 48])
        modc = sb("modc", [P, 16])
        zero = sb("zero", [P, 136])
        valid = sb("valid", [64, GRID_W])
        cut = sb("cut", [P, GRID_W], I32)
        neg = sb("neg", [P, GRID_W])
        bias_in = sb("bias_in", [HEADS * 15, 31])
        bias_rev = sb("bias_rev", [HEADS * 15, 31])
        tab_rev = sb("tab_rev", [P, TROWS, GRID_W])
        tab = sb("tab", [P, TROWS, GRID_W])
        tabi = sb("tabi", [P, WROWS, GRID_W])
        ps_x = ctx.enter_context(nc.psum_tensor("ps_x", [P, 2, KD, P], F32))
        ps_m = ctx.enter_context(nc.psum_tensor("ps_m", [P, 96], F32))
        ps_p = ctx.enter_context(nc.psum_tensor("ps_p", [P, 512], F32))

        rows_in = sig("rows_in")
        const_set = sig("const_set")
        params_turned = sig("params_turned")
        params_out = sig("params_out")
        c_sigmoid = sig("c_sigmoid")
        c_silu = sig("c_silu")
        ada_in = [sig(f"ada_in{s}") for s in range(4)]
        ada_used = sig("ada_used")
        mod_step = sig("mod_step")
        x_in = [sig(f"x_in{s}") for s in range(3)]
        x_squared = sig("x_squared")
        x_turned = sig("x_turned")
        x_evicted = sig("x_evicted")
        xt_stored = [sig(f"xt_stored{i}") for i in range(2)]
        root = sig("root")
        inverse = sig("inverse")
        r_turned = sig("r_turned")
        r_out = sig("r_out")
        r_stored = sig("r_stored")
        pad_dma = env.pad_dma
        cut_set = sig("cut_set")
        bias_loaded, bias_turned, tab_turned = sig("bias_loaded"), sig("bias_turned"), sig("tab_turned")
        tab_in = env.tab_in
        tab_cut = sig("tab_cut")
        tab_inner = sig("tab_inner")
        tab_stored = env.tab_stored

        n_ada = 6 * D // SC
        toks = TT + CTX // P
        xsrc = [io["x"][0, t * P:(t + 1) * P, :] if t < TT else io["ctx"][0, (t - TT) * P:(t - TT + 1) * P, :]
                for t in range(toks)]
        param = env.param
        row_view = lambda a, n: a.rearrange("(r c) -> r c", c=P)

        block = ctx.enter_context(nc.Block())

        @block.sync
        def _(sp):
            sp.dma_start(bias_in[:], io["rpb"][0].rearrange("h r c -> (h r) c")).then_inc(bias_loaded.sem, 16)
            r = 0
            for a in (io["b_ada"][0], io["g_pre_mix"][0], io["g_post_mix"][0], io["g_pre_ffn"][0],
                      io["g_post_ffn"][0], io["c"][0], io["c_ctx"],
                      io["w_short_conv"][0].rearrange("t c -> (t c)")):
                n = a.shape[0] // P
                sp.dma_start(rows1[r:r + n, :], row_view(a, n)).then_inc(rows_in.sem, 16)
                r += n
            sp.dma_start(rows2[0:66, :], row_view(io["w_ffn_conv"][0].rearrange("t c -> (t c)"), 66)).then_inc(rows_in.sem, 16)
            sp.dma_start(rows2[66:88, :], row_view(io["b_ffn_conv"][0], 22)).then_inc(rows_in.sem, 16)
            for n in range(max(n_ada, toks)):
                if n < toks:
                    if n >= 3:
                        sp.wait_ge(x_turned.sem, x_turned.d.next(sp))
                        sp.wait_ge(x_squared.sem, x_squared.d.next(sp))
                    sp.dma_start(xr[:, n % 3, :], xsrc[n]).then_inc(x_in[n % 3].sem, 16)
                if n < n_ada:
                    if n >= 4:
                        sp.wait_ge(ada_used.sem, ada_used.d.next(sp))
                    sp.dma_start(aw[:, n % 4, :].rearrange("p (k c) -> p k c", k=KD),
                                 slab(io["w_ada"][0], KD, n * SC, SC)).then_inc(ada_in[n % 4].sem, 16)
            sp.wait_ge(r_out.sem, r_out.d.next(sp))
            sp.dma_start(env.r_d[0:NTOK].rearrange("(t p) -> t p", p=P), rrow[:]).then_inc(r_stored.sem, 16)
            sp.wait_ge(r_stored.sem, r_stored.d.next(sp, 16))

        @block.gpsimd
        def _(pool):
            pool.memset(env.ident[:], 1.0).then_inc(const_set.sem, 1)
            pool.memset(env.ones[:], 1.0).then_inc(const_set.sem, 1)
            pool.memset(env.eps[:], EPS).then_inc(const_set.sem, 1)
            pool.memset(zero[:], 0.0).then_inc(const_set.sem, 1)
            pool.memset(valid[:], 1.0).then_inc(const_set.sem, 1)
            pool.memset(neg[:], NEG).then_inc(const_set.sem, 1)
            pool.wait_ge(const_set.sem, const_set.d.next(pool, 6))
            pool.affine_select(out=env.ident[:], in_=env.ident[:], compare_op=ALU.is_equal, fill=0.0, base=0,
                               pattern=[[-1, P]], channel_multiplier=1).then_inc(const_set.sem, 1)
            c0 = GRID_W - WIN_W
            pool.affine_select(out=valid[:, 0:c0], in_=valid[:, 0:c0], compare_op=ALU.is_ge, fill=0.0,
                               base=WIN_W // 2, pattern=[[1, c0]], channel_multiplier=-1).then_inc(const_set.sem, 1)
            pool.wait_ge(const_set.sem, const_set.d.next(pool, 2))
            pool.affine_select(out=valid[:, WIN_W:GRID_W], in_=valid[:, WIN_W:GRID_W], compare_op=ALU.is_ge,
                               fill=0.0, base=WIN_W // 2 - 1 - WIN_W, pattern=[[-1, c0]],
                               channel_multiplier=1).then_inc(const_set.sem, 1)
            pool.dma_start(env.pad_d.rearrange("h r c -> (h r c)").rearrange("(p f) -> p f", p=P),
                           zero[:]).then_inc(pad_dma.sem, 16)
            pool.wait_ge(pad_dma.sem, pad_dma.d.next(pool, 16))
            pool.wait_ge(bias_turned.sem, bias_turned.d.next(pool))
            for h in range(HEADS):
                pool.dma_start(env.pad_d[h, 1:16, 48:79], bias_rev[h * 15:(h + 1) * 15, :]).then_inc(pad_dma.sem, 16)
            pool.wait_ge(cut_set.sem, cut_set.d.next(pool))
            pool.dma_start(cut[64:128, :], cut[0:64, :]).then_inc(pad_dma.sem, 16)
            pool.wait_ge(pad_dma.sem, pad_dma.d.next(pool, 16 * (HEADS + 1)))
            for h in range(HEADS):
                if h >= 1:
                    pool.wait_ge(tab_stored.sem, tab_stored.d.next(pool, 32))
                for half in range(2):
                    pool.dma_start(tab_rev[64 * half:64 * half + 64, :, :],
                                   bass.AP(tensor=env.pad_d.tensor, offset=h * 17 * P + (1 - half) * P,
                                           ap=[[1, 64], [P, TROWS], [1, GRID_W]])).then_inc(tab_in.sem, 16)
                pool.wait_ge(tab_cut.sem, tab_cut.d.next(pool))
                pool.dma_start(env.bt_d[h, :, 0:TROWS * GRID_W],
                               tab[:].rearrange("p a b -> p (a b)")).then_inc(tab_stored.sem, 16)
                pool.tensor_copy(tabi[:], tab[:, 3:3 + WROWS, :]).then_inc(tab_inner.sem, 1)
                pool.wait_ge(tab_inner.sem, tab_inner.d.next(pool))
                pool.memset(tabi[0:64, 8:10, :], NEG).then_inc(tab_inner.sem, 1)
                pool.memset(tabi[64:128, 9:10, :], NEG).then_inc(tab_inner.sem, 1)
                pool.memset(tabi[64:128, 0:1, :], NEG).then_inc(tab_inner.sem, 1)
                pool.wait_ge(tab_inner.sem, tab_inner.d.next(pool, 3))
                pool.dma_start(env.bt_d[h, :, TROWS * GRID_W:TCOLS],
                               tabi[:].rearrange("p a b -> p (a b)")).then_inc(tab_stored.sem, 16)
            pool.wait_ge(tab_stored.sem, tab_stored.d.next(pool, 32))

        @block.vector
        def _(dve):
            dve.wait_ge(const_set.sem, const_set.d.next(dve, 9))
            dve.tensor_scalar(cut[0:64, :], valid[:], 0.0, None, ALU.is_equal).then_inc(cut_set.sem, 1)
            dve.wait_ge(bias_loaded.sem, bias_loaded.d.next(dve, 16))
            dve.tensor_copy(bias_rev[:], bass.AP(tensor=bias_in[:].tensor, offset=bias_in[:].offset + 30,
                                                 ap=[[31, HEADS * 15], [-1, 31]])).then_inc(bias_turned.sem, 1)
            dve.wait_ge(params_turned.sem, params_turned.d.next(dve))
            dve.tensor_copy(param[:, 0:108], ps_p[:, 0:108]).then_inc(params_out.sem, 1)
            dve.tensor_copy(param[:, 108:196], ps_p[:, 108:196]).then_inc(params_out.sem, 1)
            dve.wait_ge(c_sigmoid.sem, c_sigmoid.d.next(dve))
            dve.wait_ge(params_out.sem, params_out.d.next(dve, 2))
            dve.tensor_tensor(csil[:], csig[:], param[:, 80:96], ALU.mult).then_inc(c_silu.sem, 1)
            dve.wait_ge(pad_dma.sem, pad_dma.d.next(dve, 16 * (HEADS + 2)))

            def turn(t):
                dve.wait_ge(x_turned.sem, x_turned.d.next(dve))
                if t % 4 == 0 and t >= 8:
                    dve.wait_ge(xt_stored[(t // 4) % 2].sem, xt_stored[(t // 4) % 2].d.next(dve, 16))
                dve.tensor_copy(xts[:, (t // 4) % 2, :, (t % 4) * P:(t % 4 + 1) * P],
                                ps_x[:, t % 2, :, :]).then_inc(x_evicted.sem, 1)

            def table(h):
                dve.wait_ge(tab_in.sem, tab_in.d.next(dve, 32))
                back = bass.AP(tensor=tab_rev[:].tensor, offset=tab_rev[:].offset + GRID_W - 1,
                               ap=[[TROWS * GRID_W, P], [GRID_W, TROWS], [-1, GRID_W]])
                dve.tensor_copy(tab[:], back).then_inc(tab_turned.sem, 1)
                dve.wait_ge(tab_turned.sem, tab_turned.d.next(dve))
                dve.copy_predicated(tab[:], cut[:].unsqueeze(1).broadcast_to([P, TROWS, GRID_W]),
                                    neg[:].unsqueeze(1).broadcast_to([P, TROWS, GRID_W])).then_inc(tab_cut.sem, 1)

            for t in range(toks):
                turn(t)
                if t % 2 == 1 and t // 2 < HEADS:
                    table(t // 2)
            dve.wait_ge(root.sem, root.d.next(dve))
            dve.reciprocal(rr[:], rt[:]).then_inc(inverse.sem, 1)
            dve.wait_ge(r_turned.sem, r_turned.d.next(dve))
            dve.tensor_copy(rrow[:], ps_p[0:18, 256:384]).then_inc(r_out.sem, 1)
            dve.wait_ge(ada_used.sem, ada_used.d.next(dve, n_ada))
            mv = ps_m[:].rearrange("p (m s) -> p s m", s=2)
            dve.tensor_tensor(modt[:], mv[:, 0, :], param[:, 0:48], ALU.add).then_inc(mod_step.sem, 1)
            dve.tensor_tensor(modc[:], mv[:, 1, 0:16], param[:, 0:16], ALU.add).then_inc(mod_step.sem, 1)
            dve.wait_ge(mod_step.sem, mod_step.d.next(dve, 2))
            dve.tensor_copy(env.shift1[:], modt[:, 0:8])
            dve.scalar_tensor_tensor(out=env.scale1[:], in0=modt[:, 8:16], scalar=1.0, in1=param[:, 48:56],
                                     op0=ALU.add, op1=ALU.mult)
            dve.tensor_copy(env.shiftc[:], modc[:, 0:8])
            dve.scalar_tensor_tensor(out=env.scalec[:], in0=modc[:, 8:16], scalar=1.0, in1=param[:, 48:56],
                                     op0=ALU.add, op1=ALU.mult)
            dve.tensor_tensor(env.gate1[:], modt[:, 16:24], param[:, 56:64], ALU.mult)
            dve.tensor_copy(env.shift2[:], modt[:, 24:32])
            dve.scalar_tensor_tensor(out=env.scale2[:], in0=modt[:, 32:40], scalar=1.0, in1=param[:, 64:72],
                                     op0=ALU.add, op1=ALU.mult)
            dve.tensor_tensor(env.gate2[:], modt[:, 40:48], param[:, 72:80], ALU.mult).then_inc(mod_step.sem, 1)

        @block.scalar
        def _(act):
            act.wait_ge(params_out.sem, params_out.d.next(act, 2))
            act.activation(csig[:], param[:, 80:96], ACT.Sigmoid).then_inc(c_sigmoid.sem, 1)
            for t in range(toks):
                act.wait_ge(x_in[t % 3].sem, x_in[t % 3].d.next(act, 16))
                if t >= 1:
                    act.wait_ge(x_squared.sem, x_squared.d.next(act))
                act.activation(sq[:], xr[:, t % 3, :], ACT.Square, accum_out=ss[:, t:t + 1]).then_inc(x_squared.sem, 1)
                if t % 4 == 3 or t == toks - 1:
                    g = t // 4
                    cols = (t % 4 + 1) * P
                    act.wait_ge(x_evicted.sem, x_evicted.d.next(act, t % 4 + 1))
                    act.dma_start(env.xt_d.rearrange("(k p) t -> p k t", p=P)[:, :, g * NT:g * NT + cols],
                                  xts[:, g % 2, :, 0:cols]).then_inc(xt_stored[g % 2].sem, 16)
            act.wait_ge(x_squared.sem, x_squared.d.next(act))
            act.wait_ge(const_set.sem, const_set.d.next(act, 9))
            act.activation(rt[:], ss[:], ACT.Sqrt, scale=1.0 / D, bias=env.eps[:, 0:1]).then_inc(root.sem, 1)
            act.wait_ge(xt_stored[0].sem, xt_stored[0].d.next(act, 16 * 3))
            act.wait_ge(xt_stored[1].sem, xt_stored[1].d.next(act, 16 * 2))

        @block.tensor
        def _(pe):
            pe.wait_ge(const_set.sem, const_set.d.next(pe, 9))
            pe.wait_ge(rows_in.sem, rows_in.d.next(pe, 16 * 10))
            pe.transpose(ps_p[:, 0:108], rows1[:], env.ident[0:108, 0:108])
            pe.transpose(ps_p[:, 108:196], rows2[:], env.ident[0:88, 0:88]).then_inc(params_turned.sem, 1)

            def turn(t):
                pe.wait_ge(x_in[t % 3].sem, x_in[t % 3].d.next(pe, 16))
                if t >= 2:
                    pe.wait_ge(x_evicted.sem, x_evicted.d.next(pe))
                for k in range(KD):
                    last = pe.transpose(ps_x[:, t % 2, k, :], xr[:, t % 3, k * P:(k + 1) * P], env.ident[:])
                last.then_inc(x_turned.sem, 1)

            cs = csil[:].rearrange("p (s k) -> p k s", s=2)

            def ada(n):
                pe.wait_ge(ada_in[n % 4].sem, ada_in[n % 4].d.next(pe, 16))
                w = aw[:, n % 4, :].rearrange("p (k c) -> p k c", k=KD)
                for c in range(SC // P):
                    m = n * (SC // P) + c
                    for k in range(KD):
                        last = pe.matmul(ps_m[:, 2 * m:2 * m + 2], w[:, k, c * P:(c + 1) * P], cs[:, k, :],
                                         start=(k == 0), stop=(k == KD - 1))
                last.then_inc(ada_used.sem, 1)

            for n in range(max(n_ada, toks)):
                if n < toks:
                    turn(n)
                if n == 0:
                    pe.wait_ge(c_silu.sem, c_silu.d.next(pe))
                if n < n_ada:
                    ada(n)
            pe.wait_ge(inverse.sem, inverse.d.next(pe))
            pe.transpose(ps_p[0:18, 256:384], rr[:], env.ident[:]).then_inc(r_turned.sem, 1)



class Ring:

    def __init__(self, env):
        self.loaded = [Signal(env, f"w_loaded{s}") for s in range(RING)]
        self.rounded = [Signal(env, f"w_rounded{s}") for s in range(RING)]
        self.asked = Signal(env, "w_asked")
        self.ready = [Signal(env, f"w_ready{s}", 1) for s in range(RING)]

    def tensors(self, nc, ctx, tag):
        sb = lambda n, d: [ctx.enter_context(nc.sbuf_tensor(f"{n}{s}_{tag}", [P, SLAB], d)) for s in range(RING)]
        self.stage, self.hi, self.lo = sb("w_stage", F32), sb("w_hi", F32R), sb("w_lo", F32R)

    def load(self, sp, s, src):
        kc, cols = src.shape[1], src.shape[2]
        sp.wait_ge(self.ready[s].sem, self.ready[s].f.next(sp))
        sp.sem_inc(self.asked.sem, 1)
        sp.dma_start(self.stage[s][:, 0:kc * cols].rearrange("p (k c) -> p k c", k=kc),
                     src).then_inc(self.loaded[s].sem, 16)

    def round(self, act, s, words=SLAB):
        act.wait_ge(self.loaded[s].sem, self.loaded[s].d.next(act, 16))
        act.activation(self.hi[s][:, 0:words], self.stage[s][:, 0:words], ACT.Copy).then_inc(self.rounded[s].sem, 1)

    def rest(self, dve, s, words=SLAB):
        dve.wait_ge(self.rounded[s].sem, self.rounded[s].d.next(dve))
        dve.tensor_tensor(self.lo[s][:, 0:words], self.stage[s][:, 0:words],
                          self.hi[s][:, 0:words].bitcast(F32), ALU.subtract).then_inc(self.ready[s].sem, 1)

    def per(self, counts, what):
        out = {}
        for s, n in enumerate(counts):
            out.update({"load": {self.ready[s].f: n},
                        "round": {self.loaded[s].d: 16 * n},
                        "rest": {self.rounded[s].d: n},
                        "use": {self.ready[s].d: n}}[what])
        return out


class HLoad:

    def __init__(self, env):
        self.r_in = Signal(env, "h_r_in")
        self.x_in = [Signal(env, f"h_x_in{s}") for s in range(4)]
        self.normed = Signal(env, "h_normed")
        self.modulated = Signal(env, "h_modulated")
        self.rounded = Signal(env, "h_rounded")
        self.ready = Signal(env, "h_ready")
        self.edge = Signal(env, "h_edge")

    def plan(self, b):
        if b is None:
            return SEQ, CTX, 0
        return (0, BLK + 1, 1) if b == 0 else (b * BLK - 1, BLK + 1, 0)

    def load(self, sp, b, src, rsrc, rbuf, xbuf):
        t0, n, c0 = self.plan(b)
        sp.dma_start(rbuf[:, 0:n], rsrc[t0:t0 + n].partition_broadcast(P)).then_inc(self.r_in.sem, 16)
        for k in range(KD):
            if k >= 4:
                sp.wait_ge(self.ready.sem, self.ready.d.next(sp))
            sp.dma_start(xbuf[k % 4][:, 0:n], src[k * P:(k + 1) * P, t0:t0 + n]).then_inc(self.x_in[k % 4].sem, 16)
        self.ready.d.skip(sp, 4)

    def vector(self, dve, b, rbuf, xbuf, hhi, hlo):
        t0, n, c0 = self.plan(b)

        def rest(k):
            dve.wait_ge(self.rounded.sem, self.rounded.d.next(dve))
            dve.tensor_tensor(hlo[:, k, c0:c0 + n], xbuf[k % 4][:, 0:n], hhi[:, k, c0:c0 + n].bitcast(F32),
                              ALU.subtract).then_inc(self.ready.sem, 1)

        dve.wait_ge(self.r_in.sem, self.r_in.d.next(dve, 16))
        for k in range(KD):
            dve.wait_ge(self.x_in[k % 4].sem, self.x_in[k % 4].d.next(dve, 16))
            dve.tensor_tensor(xbuf[k % 4][:, 0:n], xbuf[k % 4][:, 0:n], rbuf[:, 0:n],
                              ALU.mult).then_inc(self.normed.sem, 1)
            if k >= 1:
                rest(k - 1)
        rest(KD - 1)

    def scalar(self, act, b, scale, shift, xbuf, hhi):
        t0, n, c0 = self.plan(b)
        for k in range(KD):
            act.wait_ge(self.normed.sem, self.normed.d.next(act))
            act.activation(xbuf[k % 4][:, 0:n], xbuf[k % 4][:, 0:n], ACT.Identity, scale=scale[:, k:k + 1],
                           bias=shift[:, k:k + 1]).then_inc(self.modulated.sem, 1)
            act.wait_ge(self.modulated.sem, self.modulated.d.next(act))
            act.activation(hhi[:, k, c0:c0 + n], xbuf[k % 4][:, 0:n], ACT.Copy).then_inc(self.rounded.sem, 1)

    def edges(self, pool, b, hhi, hlo):
        c = 0 if b == 0 else HW - 1
        pool.memset(hhi[:, :, c:c + 1].bitcast(F32), 0.0).then_inc(self.edge.sem, 1)
        pool.memset(hlo[:, :, c:c + 1].bitcast(F32), 0.0).then_inc(self.edge.sem, 1)

    def chunk_wait(self, pe, b):
        def wait(k):
            if k == 0 and b is not None:
                pe.wait_ge(self.edge.sem, self.edge.d.next(pe, 2))
            pe.wait_ge(self.ready.sem, self.ready.d.next(pe))
        return wait


def make_projection_signals(env):
    s = Env()
    s.qk_done, s.qk_out = Signal(env, "qk_done"), Signal(env, "qk_out", 4)
    s.v_done, s.v_out = Signal(env, "v_done"), Signal(env, "v_out", 4)
    s.o_stored = [Signal(env, f"o_stored{i}", 16) for i in range(2)]
    s.cg_done, s.cg_out = Signal(env, "cg_done"), Signal(env, "cg_out", 3)
    s.hv_done, s.hv_out = Signal(env, "hv_done"), Signal(env, "hv_out", 3)
    s.bg_done, s.bg_out = Signal(env, "bg_done"), Signal(env, "bg_out", 2)
    s.conv_step = Signal(env, "conv_step")
    s.u_rounded, s.u_ready = Signal(env, "u_rounded"), Signal(env, "u_ready")
    s.gb_done, s.gb_out = Signal(env, "gb_done"), Signal(env, "gb_out", 4)
    s.yb_done, s.yb_out = Signal(env, "yb_done"), Signal(env, "yb_out", 2)
    s.ga_done, s.ga_out = Signal(env, "ga_done"), Signal(env, "ga_out", 2)
    s.cb_stored = [Signal(env, f"cb_stored{i}", 16) for i in range(2)]
    return s


def projections(nc, env, io, b):
    ring, hl, s = env.ring, env.hload, env.psig
    n_tok = CTX if b is None else BLK
    t0 = SEQ if b is None else b * BLK
    c0 = 0 if b is None else 1
    tag = f"p{b}"
    w_in = io["w_in"][0]
    with ExitStack() as ctx:
        sb = lambda n, s, d=F32: ctx.enter_context(nc.sbuf_tensor(f"{n}_{tag}", s, d))
        ring.tensors(nc, ctx, tag)
        hhi = sb("h_hi", [P, KD, HW], F32R)
        hlo = sb("h_lo", [P, KD, HW], F32R)
        uhi = sb("u_hi", [P, KA, BLK], F32R)
        ulo = sb("u_lo", [P, KA, BLK], F32R)
        tmp = [sb(f"tmp{i}", [P, HW]) for i in range(4)]
        rbuf = sb("rbuf", [P, HW])
        ostage = [sb(f"ostage{i}", [P, BLK]) for i in range(2)]
        ps = ctx.enter_context(nc.psum_tensor(f"ps_{tag}", [P, 8, 512], F32))

        first = 0 if b is not None else 2
        slabs = [("qk", slab(w_in, KD, j * SC, SC)) for j in range(first, 4)]
        slabs += [("v", slab(w_in, KD, 2 * ATT_W + j * SC, SC)) for j in range(2)]
        n_qkv = len(slabs)
        if b is not None:
            bg, cg, hv = (3 * ATT_W + i * CONV_W for i in range(3))
            ga = 3 * ATT_W + 3 * CONV_W
            for j in range(CONV_W // SC):
                slabs += [("conv", slab(w_in, KD, col + j * SC, SC)) for col in (cg, hv, bg)]
            for j in range(D // SC):
                slabs += [("gate", slab(w_in, KD, ga + D + j * SC, SC)),
                          ("gate", slab(io["w_branch_conv"][0], KA, j * SC, SC)),
                          ("gate", slab(w_in, KD, ga + j * SC, SC))]
        words = [x.shape[1] * x.shape[2] for _, x in slabs]
        step = min(NT, n_tok)
        nts = n_tok // step
        slot = lambda n: n % RING
        wcols = lambda c, k: slice(k * SC + c * P, k * SC + (c + 1) * P)

        block = ctx.enter_context(nc.Block())

        @block.sync
        def _(sp):
            ring.load(sp, slot(0), slabs[0][1])
            hl.load(sp, b, env.xt_d, env.r_d, rbuf, tmp)
            for n in range(1, len(slabs)):
                ring.load(sp, slot(n), slabs[n][1])

        @block.gpsimd
        def _(pool):
            if b is not None:
                hl.edges(pool, b, hhi, hlo)
            hl.ready.d.skip(pool, KD)

        @block.scalar
        def _(act):
            ring.round(act, slot(0), words[0])
            hl.scalar(act, b, env.scalec if b is None else env.scale1,
                      env.shiftc if b is None else env.shift1, tmp, hhi)
            for n in range(1, RING):
                ring.round(act, slot(n), words[n])
            for n in range(n_qkv):
                if slabs[n][0] == "qk":
                    for c in range(2):
                        act.wait_ge(s.o_stored[c].sem, s.o_stored[c].f.next(act, 16))
                        for t in range(nts):
                            act.wait_ge(s.qk_done.sem, s.qk_done.d.next(act))
                            bank = 2 * c + t if nts == 2 else 2 * (n % 2) + c
                            act.activation(ostage[c][:, t * step:(t + 1) * step], ps[:, bank, 0:step],
                                           ACT.Copy).then_inc(s.qk_out.sem, 1)
                        act.wait_ge(s.qk_out.sem, s.qk_out.d.next(act, nts))
                        row = (first + n) * SC + c * P
                        act.dma_start(env.qk_d[row:row + P, t0:t0 + n_tok],
                                      ostage[c][:, 0:n_tok]).then_inc(s.o_stored[c].sem, 16)
                else:
                    for c in range(n_tok // P):
                        act.wait_ge(s.o_stored[c % 2].sem, s.o_stored[c % 2].f.next(act, 16))
                        act.wait_ge(s.v_done.sem, s.v_done.d.next(act))
                        i = c + (n - n_qkv + 2) * (n_tok // P)
                        act.activation(ostage[c % 2][:, 0:SC], ps[:, 4 + i % 4, 0:SC],
                                       ACT.Copy).then_inc(s.v_out.sem, 1)
                        act.wait_ge(s.v_out.sem, s.v_out.d.next(act))
                        col = (n - n_qkv + 2) * SC
                        act.dma_start(env.v_d[t0 + c * P:t0 + (c + 1) * P, col:col + SC],
                                      ostage[c % 2][:, 0:SC]).then_inc(s.o_stored[c % 2].sem, 16)
                if n + RING < len(slabs):
                    ring.round(act, slot(n), words[n + RING])
            if b is None:
                for c in range(2):
                    act.wait_ge(s.o_stored[c].sem, s.o_stored[c].drained(act))
                return
            for j in range(2):
                n = n_qkv + 3 * j
                for c in range(2):
                    for t in range(3):
                        act.wait_ge(s.cg_done.sem, s.cg_done.d.next(act))
                        act.activation(tmp[c][:, t * HT:(t + 1) * HT], ps[:, t, 0:HT],
                                       ACT.Copy).then_inc(s.cg_out.sem, 1)
                ring.round(act, slot(n), words[n + RING])
                act.wait_ge(s.hv_done.sem, s.hv_done.d.next(act, 6))
                ring.round(act, slot(n + 1), words[n + 1 + RING])
                for c in range(2):
                    act.wait_ge(s.bg_out.sem, s.bg_out.d.next(act, 2))
                    act.activation(uhi[:, 2 * j + c, :], tmp[2 + c][:, 0:BLK], ACT.Copy).then_inc(s.u_rounded.sem, 1)
                ring.round(act, slot(n + 2), words[n + 2 + RING])
            n = n_qkv + 6

            def rows(a, i, c):
                return bass.AP(tensor=a.tensor, offset=(i * 2 + c) * (P * SEQ) + t0, ap=[[SEQ, P], [1, BLK]])

            def gates(i, last):
                for c in range(2):
                    for t in range(2):
                        act.wait_ge(s.gb_done.sem, s.gb_done.d.next(act))
                        act.activation(tmp[c][:, t * NT:(t + 1) * NT], ps[:, 2 * c + t, :],
                                       ACT.Sigmoid).then_inc(s.gb_out.sem, 1)
                if not last:
                    ring.round(act, slot(n), words[n])
                act.wait_ge(s.yb_done.sem, s.yb_done.d.next(act, 4))
                for c in range(2):
                    act.wait_ge(s.yb_out.sem, s.yb_out.d.next(act, 2))
                    act.dma_start(rows(env.cb_d, i, c), tmp[2 + c][:, 0:BLK]).then_inc(s.cb_stored[c].sem, 16)
                if not last:
                    ring.round(act, slot(n + 1), words[n + 1])
                for c in range(2):
                    act.wait_ge(s.o_stored[c].sem, s.o_stored[c].f.next(act, 16))
                    for t in range(2):
                        act.wait_ge(s.ga_done.sem, s.ga_done.d.next(act))
                        act.activation(ostage[c][:, t * NT:(t + 1) * NT], ps[:, 6 + t, :],
                                       ACT.Sigmoid).then_inc(s.ga_out.sem, 1)
                    act.wait_ge(s.ga_out.sem, s.ga_out.d.next(act, 2))
                    act.dma_start(rows(env.ga_d, i, c), ostage[c][:]).then_inc(s.o_stored[c].sem, 16)
                if not last:
                    ring.round(act, slot(n + 2), words[n + 2])

            with repeat(act, 3, {s.gb_done.d: 4, s.ga_done.d: 4, s.yb_done.d: 4, s.yb_out.d: 4, s.ga_out.d: 4,
                                 s.o_stored[0].f: 16, s.o_stored[1].f: 16,
                                 **ring.per((1, 1, 1), "round")}) as i:
                gates(i, False)
            gates(3, True)
            for c in range(2):
                act.wait_ge(s.o_stored[c].sem, s.o_stored[c].drained(act))
                act.wait_ge(s.cb_stored[c].sem, s.cb_stored[c].d.next(act, 16 * 4))

        @block.vector
        def _(dve):
            ring.rest(dve, slot(0), words[0])
            hl.vector(dve, b, rbuf, tmp, hhi, hlo)
            for n in range(1, RING):
                ring.rest(dve, slot(n), words[n])
            for n in range(n_qkv):
                if n + RING < len(slabs):
                    ring.rest(dve, slot(n), words[n + RING])
            if b is None:
                return
            for j in range(2):
                n = n_qkv + 3 * j
                ring.rest(dve, slot(n), words[n + RING])
                for c in range(2):
                    x, y = tmp[c], tmp[2 + c]
                    for t in range(3):
                        dve.wait_ge(s.hv_done.sem, s.hv_done.d.next(dve))
                        dve.wait_ge(s.cg_out.sem, s.cg_out.d.next(dve))
                        dve.tensor_tensor(x[:, t * HT:(t + 1) * HT], ps[:, 3 + t, 0:HT],
                                          x[:, t * HT:(t + 1) * HT], ALU.mult).then_inc(s.hv_out.sem, 1)
                    dve.wait_ge(s.hv_out.sem, s.hv_out.d.next(dve, 3))
                    tap = lambda k: env.param[:, 96 + k * KA + 2 * j + c:97 + k * KA + 2 * j + c]
                    dve.tensor_scalar(y[:, 0:BLK], x[:, 0:BLK], tap(0), None, ALU.mult).then_inc(s.conv_step.sem, 1)
                    for k in (1, 2):
                        dve.wait_ge(s.conv_step.sem, s.conv_step.d.next(dve))
                        dve.scalar_tensor_tensor(out=y[:, 0:BLK], in0=x[:, k:k + BLK], scalar=tap(k),
                                                 in1=y[:, 0:BLK], op0=ALU.mult,
                                                 op1=ALU.add).then_inc(s.conv_step.sem, 1)
                    dve.wait_ge(s.conv_step.sem, s.conv_step.d.next(dve))
                ring.rest(dve, slot(n + 1), words[n + 1 + RING])
                for c in range(2):
                    y = tmp[2 + c]
                    for t in range(2):
                        dve.wait_ge(s.bg_done.sem, s.bg_done.d.next(dve))
                        dve.tensor_tensor(y[:, t * NT:(t + 1) * NT], ps[:, 6 + t, :], y[:, t * NT:(t + 1) * NT],
                                          ALU.mult).then_inc(s.bg_out.sem, 1)
                for c in range(2):
                    dve.wait_ge(s.u_rounded.sem, s.u_rounded.d.next(dve))
                    dve.tensor_tensor(ulo[:, 2 * j + c, :], tmp[2 + c][:, 0:BLK],
                                      uhi[:, 2 * j + c, :].bitcast(F32), ALU.subtract).then_inc(s.u_ready.sem, 1)
                ring.rest(dve, slot(n + 2), words[n + 2 + RING])
            n = n_qkv + 6

            def gates(last):
                if not last:
                    ring.rest(dve, slot(n), words[n])
                for c in range(2):
                    dve.wait_ge(s.cb_stored[c].sem, s.cb_stored[c].f.next(dve, 16))
                    for t in range(2):
                        dve.wait_ge(s.gb_out.sem, s.gb_out.d.next(dve))
                        dve.wait_ge(s.yb_done.sem, s.yb_done.d.next(dve))
                        dve.tensor_tensor(tmp[2 + c][:, t * NT:(t + 1) * NT], ps[:, 4 + t, :],
                                          tmp[c][:, t * NT:(t + 1) * NT], ALU.mult).then_inc(s.yb_out.sem, 1)
                if not last:
                    ring.rest(dve, slot(n + 1), words[n + 1])
                    ring.rest(dve, slot(n + 2), words[n + 2])

            with repeat(dve, 3, {s.gb_out.d: 4, s.yb_done.d: 4, s.cb_stored[0].f: 16, s.cb_stored[1].f: 16,
                                 **ring.per((1, 1, 1), "rest")}):
                gates(False)
            gates(True)

        @block.tensor
        def _(pe):
            chunk_wait = hl.chunk_wait(pe, b)

            def channel_tile(n, c, bank, a0, cols, kc, ahi, alo, done):
                w = slot(n)
                product(pe, ps[:, bank, 0:cols],
                        lambda k: (ring.hi[w][:, wcols(c, k)], ring.lo[w][:, wcols(c, k)]),
                        lambda k: (ahi[:, k, a0:a0 + cols], alo[:, k, a0:a0 + cols]),
                        kc).then_inc(done.sem, 1)

            def first_tile(c, t):
                a = slice(c0 + t * step, c0 + (t + 1) * step)
                return (ps[:, 2 * c + t if nts == 2 else c, 0:step],
                        lambda k: (ring.hi[0][:, wcols(c, k)], ring.lo[0][:, wcols(c, k)]),
                        lambda k: (hhi[:, k, a], hlo[:, k, a]), s.qk_done)

            pe.wait_ge(ring.ready[0].sem, ring.ready[0].d.next(pe))
            pe.wait_ge(s.qk_out.sem, s.qk_out.f.next(pe, 2 * nts))
            products_together(pe, [first_tile(c, t) for c in range(2) for t in range(nts)], KD, chunk_wait)
            for n in range(1, n_qkv):
                pe.wait_ge(ring.ready[slot(n)].sem, ring.ready[slot(n)].d.next(pe))
                if slabs[n][0] == "qk":
                    for c in range(2):
                        for t in range(nts):
                            pe.wait_ge(s.qk_out.sem, s.qk_out.f.next(pe))
                            bank = 2 * c + t if nts == 2 else 2 * (n % 2) + c
                            channel_tile(n, c, bank, c0 + t * step, step, KD, hhi, hlo, s.qk_done)
                else:
                    for c in range(n_tok // P):
                        pe.wait_ge(s.v_out.sem, s.v_out.f.next(pe))
                        i = c + (n - n_qkv + 2) * (n_tok // P)
                        w = slot(n)
                        a = slice(c0 + c * P, c0 + (c + 1) * P)
                        product(pe, ps[:, 4 + i % 4, 0:SC],
                                lambda k: (hhi[:, k, a], hlo[:, k, a]),
                                lambda k: (ring.hi[w][:, k * SC:(k + 1) * SC], ring.lo[w][:, k * SC:(k + 1) * SC]),
                                KD).then_inc(s.v_done.sem, 1)
            if b is None:
                return
            pe.wait_ge(s.qk_out.sem, s.qk_out.drained(pe))
            pe.wait_ge(s.v_out.sem, s.v_out.drained(pe))
            for j in range(2):
                n = n_qkv + 3 * j
                pe.wait_ge(s.bg_out.sem, s.bg_out.drained(pe))
                for m, (done, out, bank, tiles, a0, cols) in enumerate((
                        (s.cg_done, s.cg_out, 0, 3, 0, HT), (s.hv_done, s.hv_out, 3, 3, 0, HT),
                        (s.bg_done, s.bg_out, 6, 2, 1, NT))):
                    pe.wait_ge(ring.ready[slot(n + m)].sem, ring.ready[slot(n + m)].d.next(pe))
                    for c in range(2):
                        for t in range(tiles):
                            pe.wait_ge(out.sem, out.f.next(pe))
                            channel_tile(n + m, c, bank + t, a0 + t * cols, cols, KD, hhi, hlo, done)
            for x in (s.cg_out, s.hv_out, s.bg_out):
                pe.wait_ge(x.sem, x.drained(pe))
            pe.wait_ge(s.u_ready.sem, s.u_ready.d.next(pe, 4))
            n = n_qkv + 6
            with repeat(pe, 4, {s.gb_out.f: 4, s.yb_out.f: 4, s.ga_out.f: 4, **ring.per((1, 1, 1), "use")}):
                pe.wait_ge(s.yb_out.sem, s.yb_out.drained(pe))
                for m, (done, out, bank, kc, a0, ahi, alo) in enumerate((
                        (s.gb_done, s.gb_out, 0, KD, 1, hhi, hlo), (s.yb_done, s.yb_out, 4, KA, 0, uhi, ulo),
                        (s.ga_done, s.ga_out, 6, KD, 1, hhi, hlo))):
                    pe.wait_ge(ring.ready[slot(n + m)].sem, ring.ready[slot(n + m)].d.next(pe))
                    for c in range(2):
                        for t in range(2):
                            pe.wait_ge(out.sem, out.f.next(pe))
                            channel_tile(n + m, c, bank + (2 * c if m == 0 else 0) + t, a0 + t * NT, NT, kc,
                                         ahi, alo, done)


def make_attention_signals(env):
    s = Env()
    s.q_in, s.k_in, s.v_in = Signal(env, "q_in"), Signal(env, "k_in"), Signal(env, "v_in")
    s.tab_in = [Signal(env, f"att_tab_in{i}") for i in range(2)]
    s.q_rounded, s.k_rounded, s.v_rounded = (Signal(env, n) for n in ("q_rounded", "k_rounded", "v_rounded"))
    s.q_split, s.k_split, s.v_split = (Signal(env, n) for n in ("q_split", "k_split", "v_split"))
    s.zeroed = Signal(env, "att_zeroed")
    s.scored = Signal(env, "scored")
    s.biased = Signal(env, "biased", 2)
    s.peaked = Signal(env, "peaked")
    s.edge_step = Signal(env, "edge_step")
    s.score_seen = Signal(env, "score_seen")
    s.exped = Signal(env, "exped")
    s.turned = Signal(env, "turned")
    s.p_rounded = Signal(env, "p_rounded")
    s.p_split = Signal(env, "p_split", 1)
    s.summed = Signal(env, "summed")
    s.weighed = Signal(env, "weighed")
    s.low_out = Signal(env, "low_out")
    s.o_out = Signal(env, "att_o_out", 2)
    s.att_stored = [Signal(env, f"att_stored{i}", 16) for i in range(2)]
    return s


def attention(nc, env):
    s = env.asig
    nk = NTOK // P
    width = WIN + CTX
    zero0 = TCOLS

    def span(n):
        r = 2 * n
        if r < WIN_H // 2:
            return 0, WIN_H - 1 - r, WIN_H * GRID_W
        if r > ROWS - WIN_H // 2 - 2:
            return ROWS - WIN_H, ROWS - 1 - r, WIN_H * GRID_W
        return r - WIN_H // 2, None, WIN

    with ExitStack() as ctx:
        sb = lambda n, sh, d=F32: ctx.enter_context(nc.sbuf_tensor("att_" + n, sh, d))
        qr, kr, vr = sb("qr", [P, SEQ]), sb("kr", [P, NTOK]), sb("vr", [P, nk, DH])
        qhi = [sb(f"qhi{i}", [P, SEQ], F32R) for i in range(2)]
        qlo = [sb(f"qlo{i}", [P, SEQ], F32R) for i in range(2)]
        kk = [sb(f"kk{i}", [P, NTOK], F32R) for i in range(2)]
        vv = [sb(f"vv{i}", [P, nk, 2 * DH], F32R) for i in range(2)]
        tab = [sb(f"tab{i}", [P, TCOLS + CTX]) for i in range(2)]
        sc = [sb(f"sc{i}", [P, width]) for i in range(2)]
        pthi = [sb(f"pthi{i}", [P, width], F32R) for i in range(2)]
        ptlo = [sb(f"ptlo{i}", [P, width], F32R) for i in range(2)]
        peak, peak2, npeak = sb("peak", [P, 32]), sb("peak2", [P, 32]), sb("npeak", [P, 32])
        den, rden = sb("den", [P, 32]), sb("rden", [P, 32])
        low = sb("low", [P, 2, DH])
        out = [sb(f"out{i}", [P, PAIRS, DH]) for i in range(2)]
        ps_s = ctx.enter_context(nc.psum_tensor("ps_s", [P, 2, 1024], F32))
        ps_t = ctx.enter_context(nc.psum_tensor("ps_t", [P, 1024], F32))
        ps_o = ctx.enter_context(nc.psum_tensor("ps_o", [P, 2, 512], F32))
        block = ctx.enter_context(nc.Block())

        @block.gpsimd
        def _(pool):
            for i in range(2):
                pool.memset(tab[i][:, zero0:zero0 + CTX], 0.0).then_inc(s.zeroed.sem, 1)

        @block.sync
        def _(sp):
            for h in range(HEADS):
                if h >= 1:
                    sp.wait_ge(s.q_split.sem, s.q_split.d.next(sp))
                    sp.wait_ge(s.k_split.sem, s.k_split.d.next(sp))
                    sp.wait_ge(s.v_split.sem, s.v_split.d.next(sp))
                for half in (0, 64):
                    sp.dma_start(qr[half:half + 64, :], env.qk_d[h * DH:(h + 1) * DH, 0:SEQ]).then_inc(s.q_in.sem, 16)
                for half in (0, 64):
                    sp.dma_start(kr[half:half + 64, :],
                                 env.qk_d[ATT_W + h * DH:ATT_W + (h + 1) * DH, :]).then_inc(s.k_in.sem, 16)
                sp.dma_start(vr[:], env.v_d[:, h * DH:(h + 1) * DH].rearrange("(t p) d -> p t d", p=P)).then_inc(s.v_in.sem, 16)
                if h >= 2:
                    sp.wait_ge(s.biased.sem, s.biased.d.next(sp, PAIRS))
                sp.dma_start(tab[h % 2][:, 0:TCOLS], env.bt_d[h]).then_inc(s.tab_in[h % 2].sem, 16)
            sp.wait_ge(s.biased.sem, s.biased.d.next(sp, 2 * PAIRS))

        def round_q(act, i):
            act.wait_ge(s.q_in.sem, s.q_in.d.next(act, 32))
            act.activation(qhi[i][:], qr[:], ACT.Copy, scale=DH ** -0.5).then_inc(s.q_rounded.sem, 1)

        def round_k(act, i):
            act.wait_ge(s.k_in.sem, s.k_in.d.next(act, 32))
            act.activation(kk[i][:], kr[:], ACT.Copy).then_inc(s.k_rounded.sem, 1)

        def round_v(act, i):
            act.wait_ge(s.v_in.sem, s.v_in.d.next(act, 16))
            act.activation(vv[i][:, :, 0:DH], vr[:], ACT.Copy).then_inc(s.v_rounded.sem, 1)

        def rest_q(dve, i):
            dve.wait_ge(s.q_rounded.sem, s.q_rounded.d.next(dve))
            dve.scalar_tensor_tensor(out=qlo[i][:], in0=qr[:], scalar=DH ** -0.5, in1=qhi[i][:].bitcast(F32),
                                     op0=ALU.mult, op1=ALU.subtract).then_inc(s.q_split.sem, 1)

        def rest_k(dve, i):
            dve.wait_ge(s.k_rounded.sem, s.k_rounded.d.next(dve))
            dve.tensor_tensor(kk[i][64:128, :], kr[64:128, :], kk[i][64:128, :].bitcast(F32),
                              ALU.subtract).then_inc(s.k_split.sem, 1)

        def rest_v(dve, i):
            dve.wait_ge(s.v_rounded.sem, s.v_rounded.d.next(dve))
            dve.tensor_tensor(vv[i][:, :, DH:2 * DH], vr[:], vv[i][:, :, 0:DH].bitcast(F32),
                              ALU.subtract).then_inc(s.v_split.sem, 1)

        @block.scalar
        def _(act):
            def expo(g):
                w = span(g % PAIRS)[2] + CTX
                act.wait_ge(s.peaked.sem, s.peaked.d.next(act))
                act.activation(sc[g % 2][:, 0:w], sc[g % 2][:, 0:w], ACT.Exp, bias=npeak[:, g:g + 1],
                               accum_out=den[:, g:g + 1]).then_inc(s.exped.sem, 1)

            def round_p(g):
                w = span(g % PAIRS)[2] + CTX
                act.wait_ge(s.turned.sem, s.turned.d.next(act))
                act.activation(pthi[g % 2][:, 0:w], ps_t[:, 0:w], ACT.Copy).then_inc(s.p_rounded.sem, 1)

            def store(h, i):
                act.wait_ge(s.o_out.sem, s.o_out.d.next(act, PAIRS))
                act.dma_start(bass.AP(tensor=env.att_d.tensor, offset=(h + i) * DH,
                                      ap=[[ATT_W, P], [P * ATT_W, PAIRS], [1, DH]]),
                              out[i][:]).then_inc(s.att_stored[i].sem, 16)

            def two_heads(h, last):
                expo(0)
                for g in range(2 * PAIRS):
                    nxt = (g // PAIRS + 1) % 2
                    if not (last and g >= PAIRS):
                        if g % PAIRS == 2:
                            round_q(act, nxt)
                        if g % PAIRS == 4:
                            round_k(act, nxt)
                        if g % PAIRS == 6:
                            round_v(act, nxt)
                    round_p(g)
                    if g + 1 < 2 * PAIRS:
                        expo(g + 1)
                    if g == PAIRS + 1:
                        store(h, 0)
                store(h, 1)

            round_q(act, 0)
            round_k(act, 0)
            round_v(act, 0)
            with repeat(act, HEADS // 2 - 1, {
                    s.q_in.d: 64, s.k_in.d: 64, s.v_in.d: 32, s.peaked.d: 32, s.turned.d: 32,
                    s.o_out.d: 32}) as i:
                two_heads(i * 2, False)
            two_heads(HEADS - 2, True)
            for i in range(2):
                act.wait_ge(s.att_stored[i].sem, s.att_stored[i].d.next(act, 16 * HEADS // 2))

        @block.vector
        def _(dve):
            def bias(g):
                n = g % PAIRS
                _, j, w = span(n)
                t = tab[g // PAIRS]
                dve.wait_ge(s.scored.sem, s.scored.d.next(dve))
                dve.sem_inc(s.score_seen.sem, 1)
                if j is None:
                    dve.tensor_tensor_reduce(sc[g % 2][:, 0:w + CTX], ps_s[:, g % 2, 0:w + CTX],
                                             t[:, TROWS * GRID_W:TCOLS + CTX], 1.0, NEG, ALU.add, ALU.max,
                                             peak[:, g:g + 1]).then_inc(s.biased.sem, 1)
                    dve.wait_ge(s.biased.sem, s.biased.d.next(dve))
                    dve.tensor_scalar(npeak[:, g:g + 1], peak[:, g:g + 1], -1.0, None, ALU.mult).then_inc(s.peaked.sem, 1)
                    return
                dve.tensor_tensor_reduce(sc[g % 2][:, 0:w], ps_s[:, g % 2, 0:w],
                                         t[:, j * GRID_W:j * GRID_W + w], 1.0, NEG, ALU.add, ALU.max,
                                         peak[:, g:g + 1]).then_inc(s.edge_step.sem, 1)
                dve.tensor_tensor_reduce(sc[g % 2][:, w:w + CTX], ps_s[:, g % 2, w:w + CTX],
                                         t[:, zero0:zero0 + CTX], 1.0, NEG, ALU.add, ALU.max,
                                         peak2[:, g:g + 1]).then_inc(s.biased.sem, 1)
                dve.wait_ge(s.edge_step.sem, s.edge_step.d.next(dve))
                dve.wait_ge(s.biased.sem, s.biased.d.next(dve))
                dve.tensor_scalar(npeak[:, g:g + 1], peak[:, g:g + 1], peak2[:, g:g + 1], -1.0, ALU.max,
                                  ALU.mult).then_inc(s.peaked.sem, 1)

            def rest_p(g):
                w = span(g % PAIRS)[2] + CTX
                dve.wait_ge(s.p_rounded.sem, s.p_rounded.d.next(dve))
                dve.tensor_tensor(ptlo[g % 2][:, 0:w], ps_t[:, 0:w], pthi[g % 2][:, 0:w].bitcast(F32),
                                  ALU.subtract).then_inc(s.p_split.sem, 1)

            def inverse(g):
                dve.wait_ge(s.exped.sem, s.exped.d.next(dve))
                dve.reciprocal(rden[:, g:g + 1], den[:, g:g + 1]).then_inc(s.summed.sem, 1)

            def finish(g):
                i, n = g // PAIRS, g % PAIRS
                if n == 0:
                    dve.wait_ge(s.att_stored[i].sem, s.att_stored[i].f.next(dve, 16))
                dve.wait_ge(s.weighed.sem, s.weighed.d.next(dve))
                dve.wait_ge(s.summed.sem, s.summed.d.next(dve))
                dve.tensor_scalar(low[:, g % 2, :], ps_o[:, g % 2, DH:2 * DH], rden[:, g:g + 1], None,
                                  ALU.mult).then_inc(s.low_out.sem, 1)
                dve.wait_ge(s.low_out.sem, s.low_out.d.next(dve))
                dve.scalar_tensor_tensor(out=out[i][:, n, :], in0=ps_o[:, g % 2, 0:DH], scalar=rden[:, g:g + 1],
                                         in1=low[:, g % 2, :], op0=ALU.mult, op1=ALU.add).then_inc(s.o_out.sem, 1)

            def two_heads(last):
                dve.wait_ge(s.tab_in[0].sem, s.tab_in[0].d.next(dve, 16))
                bias(0)
                for g in range(2 * PAIRS):
                    nxt = (g // PAIRS + 1) % 2
                    if g + 1 < 2 * PAIRS:
                        if g + 1 == PAIRS:
                            dve.wait_ge(s.tab_in[1].sem, s.tab_in[1].d.next(dve, 16))
                        bias(g + 1)
                    if not (last and g >= PAIRS):
                        if g % PAIRS == 2:
                            rest_q(dve, nxt)
                        if g % PAIRS == 4:
                            rest_k(dve, nxt)
                        if g % PAIRS == 6:
                            rest_v(dve, nxt)
                    rest_p(g)
                    inverse(g)
                    if g >= 1:
                        finish(g - 1)
                finish(2 * PAIRS - 1)

            dve.wait_ge(s.zeroed.sem, s.zeroed.d.next(dve, 2))
            rest_q(dve, 0)
            rest_k(dve, 0)
            rest_v(dve, 0)
            with repeat(dve, HEADS // 2 - 1, {
                    s.tab_in[0].d: 16, s.tab_in[1].d: 16, s.q_rounded.d: 2, s.k_rounded.d: 2, s.v_rounded.d: 2,
                    s.scored.d: 32, s.biased.d: 32, s.edge_step.d: 8, s.p_rounded.d: 32, s.exped.d: 32,
                    s.weighed.d: 32, s.summed.d: 32, s.low_out.d: 32,
                    s.att_stored[0].f: 16, s.att_stored[1].f: 16}):
                two_heads(False)
            two_heads(True)

        @block.tensor
        def _(pe):
            def score(g):
                i, n = g // PAIRS, g % PAIRS
                row, _, w = span(n)
                if n == 0:
                    pe.wait_ge(s.q_split.sem, s.q_split.d.next(pe))
                    pe.wait_ge(s.k_split.sem, s.k_split.d.next(pe))
                    pe.wait_ge(s.v_split.sem, s.v_split.d.next(pe))
                pe.wait_ge(s.biased.sem, s.biased.f.next(pe))
                k0 = row * GRID_W
                for a, b, c in ((0, 512, k0), (512, w, k0 + 512), (w, w + CTX, SEQ)):
                    if a < b:
                        for q, first in ((qhi, True), (qlo, False)):
                            last = pe.matmul(ps_s[:, g % 2, a:b], q[i][:, n * P:(n + 1) * P],
                                             kk[i][:, c:c + b - a], start=first, stop=not first)
                last.then_inc(s.scored.sem, 1)

            def turn(g):
                w = span(g % PAIRS)[2] + CTX
                pe.wait_ge(s.exped.sem, s.exped.d.next(pe))
                pe.wait_ge(s.p_split.sem, s.p_split.f.next(pe))
                for c in range(w // P):
                    last = pe.transpose(ps_t[:, c * P:(c + 1) * P], sc[g % 2][:, c * P:(c + 1) * P], env.ident[:])
                last.then_inc(s.turned.sem, 1)

            def weigh(g):
                i, n = g // PAIRS, g % PAIRS
                row, _, w = span(n)
                tiles = [row * GRID_W // P + c for c in range(w // P)] + [SEQ // P + c for c in range(CTX // P)]
                pe.wait_ge(s.p_split.sem, s.p_split.d.next(pe))
                pe.wait_ge(s.o_out.sem, s.o_out.f.next(pe))
                for c, t in enumerate(tiles):
                    p = slice(c * P, (c + 1) * P)
                    pe.matmul(ps_o[:, g % 2, 0:2 * DH], pthi[g % 2][:, p], vv[i][:, t, :], start=(c == 0), stop=False)
                    last = pe.matmul(ps_o[:, g % 2, 0:DH], ptlo[g % 2][:, p], vv[i][:, t, 0:DH], start=False,
                                     stop=(c == len(tiles) - 1))
                last.then_inc(s.weighed.sem, 1)

            with repeat(pe, HEADS // 2, {
                    s.q_split.d: 2, s.k_split.d: 2, s.v_split.d: 2, s.biased.f: 32, s.exped.d: 32,
                    s.p_split.f: 32, s.p_split.d: 32, s.o_out.f: 32}):
                score(0)
                for g in range(2 * PAIRS):
                    if g + 1 < 2 * PAIRS:
                        score(g + 1)
                    turn(g)
                    if g >= 1:
                        weigh(g - 1)
                weigh(2 * PAIRS - 1)


class Norm:

    def __init__(self, env, name):
        self.squared = Signal(env, f"{name}_squared")
        self.added = Signal(env, f"{name}_added", 2)
        self.summed = Signal(env, f"{name}_summed")
        self.rooted = Signal(env, f"{name}_rooted")
        self.ready = Signal(env, f"{name}_ready")

    def add(self, pool, k, acc, sq):
        pool.wait_ge(self.squared.sem, self.squared.d.next(pool))
        if k == 0:
            pool.tensor_copy(acc[:], sq[:]).then_inc(self.added.sem, 1)
        else:
            pool.wait_ge(self.added.sem, self.added.d.next(pool))
            pool.tensor_tensor(acc[:], acc[:], sq[:], ALU.add).then_inc(self.added.sem, 1)
        if k == KD - 1:
            pool.wait_ge(self.added.sem, self.added.d.next(pool))

    def sums(self, pe, env, ps, banks, acc):
        pe.wait_ge(self.added.sem, self.added.d.next(pe, KD))
        for t, bank in enumerate(banks):
            last = pe.matmul(ps[:, bank, :], env.ones[:], acc[:, t * NT:(t + 1) * NT], start=True, stop=True)
        last.then_inc(self.summed.sem, 1)

    def root(self, act, env, ps, banks, r):
        act.wait_ge(self.summed.sem, self.summed.d.next(act))
        for t, bank in enumerate(banks):
            last = act.activation(r[:, t * NT:(t + 1) * NT], ps[:, bank, :], ACT.Sqrt, scale=1.0 / D,
                                  bias=env.eps[:, 0:1])
        last.then_inc(self.rooted.sem, 1)

    def inverse(self, dve, r):
        dve.wait_ge(self.rooted.sem, self.rooted.d.next(dve))
        dve.reciprocal(r[:], r[:]).then_inc(self.ready.sem, 1)


def make_merge_signals(env):
    s = Env()
    s.att_in = [Signal(env, f"m_att_in{i}") for i in range(2)]
    s.att_turned, s.att_rounded = Signal(env, "m_att_turned"), Signal(env, "m_att_rounded")
    s.att_split = Signal(env, "m_att_split", 2)
    s.gate_in = [Signal(env, f"m_gate_in{i}") for i in range(2)]
    s.ya_done, s.ya_out = Signal(env, "ya_done"), Signal(env, "ya_out", 4)
    s.z_summed, s.z_rounded = Signal(env, "z_summed"), Signal(env, "z_rounded")
    s.z_split = Signal(env, "z_split", 2)
    s.y_done, s.y_out = Signal(env, "y_done"), Signal(env, "y_out", 4)
    s.post, s.next = Norm(env, "m_post"), Norm(env, "m_next")
    s.x_in = [Signal(env, f"m_x_in{i}") for i in range(2)]
    s.y_scaled = Signal(env, "m_y_scaled")
    s.x_sum = Signal(env, "m_x_sum")
    s.stored, s.r_stored = Signal(env, "m_stored"), Signal(env, "m_r_stored")
    return s


def merge(nc, env, io, b):
    ring, s = env.ring, env.msig
    t0 = b * BLK
    tag = f"m{b}"
    WC = 4 * P
    slabs = [slab(io["w_branch_attn"][0], KA, j * WC, WC) for j in range(2)]
    slabs += [slab(io["w_out"][0], KD, j * SC, SC) for j in range(4)]
    with ExitStack() as ctx:
        sb = lambda n, sh, d=F32: ctx.enter_context(nc.sbuf_tensor(f"{n}_{tag}", sh, d))
        ring.tensors(nc, ctx, tag)
        zhi, zlo = sb("z_hi", [P, KD, BLK], F32R), sb("z_lo", [P, KD, BLK], F32R)
        atok = [sb(f"atok{i}", [P, ATT_W]) for i in range(2)]
        ga = [sb(f"ga{i}", [P, BLK]) for i in range(2)]
        cb = [sb(f"cb{i}", [P, BLK]) for i in range(2)]
        acc, r = sb("acc", [P, BLK]), sb("r", [P, BLK])
        with ExitStack() as inner:
            ahi = inner.enter_context(nc.sbuf_tensor(f"a_hi_{tag}", [P, KA, BLK], F32R))
            alo = inner.enter_context(nc.sbuf_tensor(f"a_lo_{tag}", [P, KA, BLK], F32R))
        y = sb("y", [P, KD, BLK])
        ps = ctx.enter_context(nc.psum_tensor(f"ps_{tag}", [P, 8, 512], F32))
        y_banks = (0, 1, 6, 7)
        slot = lambda n: n % RING
        block = ctx.enter_context(nc.Block())

        @block.sync
        def _(sp):
            for n in range(RING):
                ring.load(sp, slot(n), slabs[n])
            for t in range(BLK // P):
                if t >= 2:
                    sp.wait_ge(s.att_turned.sem, s.att_turned.d.next(sp))
                sp.dma_start(atok[t % 2][:], env.att_d[t0 + t * P:t0 + (t + 1) * P, :]).then_inc(s.att_in[t % 2].sem, 16)
            for k in range(KD):
                if k == 4:
                    ring.load(sp, slot(RING), slabs[RING])
                sp.wait_ge(s.z_split.sem, s.z_split.f.next(sp))
                sp.dma_start(ga[k % 2][:], env.ga_d[k * P:(k + 1) * P, t0:t0 + BLK]).then_inc(s.gate_in[k % 2].sem, 16)
                sp.dma_start(cb[k % 2][:], env.cb_d[k * P:(k + 1) * P, t0:t0 + BLK]).then_inc(s.gate_in[k % 2].sem, 16)
            sp.wait_ge(s.att_turned.sem, s.att_turned.d.next(sp, 2))
            for n in range(RING + 1, len(slabs)):
                ring.load(sp, slot(n), slabs[n])
            sp.wait_ge(s.z_split.sem, s.z_split.drained(sp))
            for k in range(KD):
                if k >= 2:
                    sp.wait_ge(s.x_sum.sem, s.x_sum.d.next(sp))
                sp.dma_start(cb[k % 2][:], env.xt_d[k * P:(k + 1) * P, t0:t0 + BLK]).then_inc(s.x_in[k % 2].sem, 16)
            sp.wait_ge(s.x_sum.sem, s.x_sum.d.next(sp, 2))

        @block.gpsimd
        def _(pool):
            for k in range(KD):
                s.post.add(pool, k, acc, ga[k % 2])
            pool.wait_ge(s.post.summed.sem, s.post.summed.d.next(pool))
            for k in range(KD):
                s.next.add(pool, k, acc, ga[k % 2])

        @block.scalar
        def _(act):
            for n in range(RING):
                ring.round(act, slot(n))
            for t in range(BLK // P):
                act.wait_ge(s.att_turned.sem, s.att_turned.d.next(act))
                act.activation(ahi[:, :, t * P:(t + 1) * P], ps[:, t % 2, :].rearrange("p (k t) -> p k t", k=KA),
                               ACT.Copy).then_inc(s.att_rounded.sem, 1)
            for k in range(KD):
                act.wait_ge(s.z_summed.sem, s.z_summed.d.next(act))
                act.activation(zhi[:, k, :], ga[k % 2][:], ACT.Copy).then_inc(s.z_rounded.sem, 1)
                if k % 4 == 3:
                    ring.round(act, slot(k // 4), SLAB)
            act.wait_ge(s.z_split.sem, s.z_split.d.next(act, KD))
            for k in range(KD):
                act.wait_ge(s.post.added.sem, s.post.added.f.next(act))
                for t in range(2):
                    act.wait_ge(s.y_done.sem, s.y_done.d.next(act))
                    bank = y_banks[(2 * k + t) % 4]
                    act.activation(y[:, k, t * NT:(t + 1) * NT], ps[:, bank, :], ACT.Copy)
                    last = act.activation(ga[k % 2][:, t * NT:(t + 1) * NT], ps[:, bank, :], ACT.Square)
                    last.then_inc(s.y_out.sem, 1)
                act.wait_ge(s.y_out.sem, s.y_out.d.next(act, 2))
                act.sem_inc(s.post.squared.sem, 1)
                if k == 1:
                    ring.round(act, slot(5), SLAB)
            s.post.root(act, env, ps, (2, 3), r)
            for k in range(KD):
                act.wait_ge(s.next.added.sem, s.next.added.f.next(act))
                if k < 2:
                    act.wait_ge(s.post.added.sem, s.post.added.d.next(act, KD // 2))
                act.wait_ge(s.x_sum.sem, s.x_sum.d.next(act))
                act.dma_start(env.x1_d[k * P:(k + 1) * P, t0:t0 + BLK], y[:, k, :]).then_inc(s.stored.sem, 16)
                act.activation(ga[k % 2][:], y[:, k, :], ACT.Square).then_inc(s.next.squared.sem, 1)
            s.next.root(act, env, ps, (2, 3), r)
            act.wait_ge(s.next.ready.sem, s.next.ready.d.next(act))
            act.dma_start(env.r2_d[t0:t0 + BLK].rearrange("(a t) -> a t", a=1), r[0:1, :]).then_inc(s.r_stored.sem, 16)
            act.wait_ge(s.stored.sem, s.stored.d.next(act, 16 * KD))
            act.wait_ge(s.r_stored.sem, s.r_stored.d.next(act, 16))

        @block.vector
        def _(dve):
            for n in range(RING):
                ring.rest(dve, slot(n))
            for t in range(BLK // P):
                dve.wait_ge(s.att_rounded.sem, s.att_rounded.d.next(dve))
                dve.tensor_tensor(alo[:, :, t * P:(t + 1) * P], ps[:, t % 2, :].rearrange("p (k t) -> p k t", k=KA),
                                  ahi[:, :, t * P:(t + 1) * P].bitcast(F32), ALU.subtract).then_inc(s.att_split.sem, 1)

            def rest_z(k):
                dve.wait_ge(s.z_rounded.sem, s.z_rounded.d.next(dve))
                dve.tensor_tensor(zlo[:, k, :], ga[k % 2][:], zhi[:, k, :].bitcast(F32),
                                  ALU.subtract).then_inc(s.z_split.sem, 1)

            for k in range(KD):
                dve.wait_ge(s.gate_in[k % 2].sem, s.gate_in[k % 2].d.next(dve, 32))
                for t in range(2):
                    dve.wait_ge(s.ya_done.sem, s.ya_done.d.next(dve))
                    dve.tensor_tensor(ga[k % 2][:, t * NT:(t + 1) * NT], ps[:, 2 + (2 * k + t) % 4, :],
                                      ga[k % 2][:, t * NT:(t + 1) * NT], ALU.mult).then_inc(s.ya_out.sem, 1)
                dve.wait_ge(s.ya_out.sem, s.ya_out.d.next(dve, 2))
                dve.tensor_tensor(ga[k % 2][:], ga[k % 2][:], cb[k % 2][:], ALU.add).then_inc(s.z_summed.sem, 1)
                rest_z(k)
                if k % 4 == 3:
                    ring.rest(dve, slot(k // 4))
            ring.rest(dve, slot(5))
            s.post.inverse(dve, r)
            dve.wait_ge(s.post.ready.sem, s.post.ready.d.next(dve))
            for k in range(KD):
                dve.wait_ge(s.x_in[k % 2].sem, s.x_in[k % 2].d.next(dve, 16))
                if k == 0:
                    dve.wait_ge(s.y_out.sem, s.y_out.d.next(dve, 2 * KD))
                dve.scalar_tensor_tensor(out=y[:, k, :], in0=y[:, k, :], scalar=env.gate1[:, k:k + 1], in1=r[:],
                                         op0=ALU.mult, op1=ALU.mult).then_inc(s.y_scaled.sem, 1)
                dve.wait_ge(s.y_scaled.sem, s.y_scaled.d.next(dve))
                dve.tensor_tensor(y[:, k, :], y[:, k, :], cb[k % 2][:], ALU.add).then_inc(s.x_sum.sem, 1)
            s.next.inverse(dve, r)

        @block.tensor
        def _(pe):
            for t in range(BLK // P):
                pe.wait_ge(s.att_in[t % 2].sem, s.att_in[t % 2].d.next(pe, 16))
                pe.wait_ge(s.att_split.sem, s.att_split.f.next(pe))
                for k in range(KA):
                    last = pe.transpose(ps[:, t % 2, k * P:(k + 1) * P], atok[t % 2][:, k * P:(k + 1) * P], env.ident[:])
                last.then_inc(s.att_turned.sem, 1)
            pe.wait_ge(s.att_split.sem, s.att_split.drained(pe))
            for n in range(2):
                pe.wait_ge(ring.ready[slot(n)].sem, ring.ready[slot(n)].d.next(pe))
                w = slot(n)
                for c in range(WC // P):
                    for t in range(2):
                        i = (n * (WC // P) + c) * 2 + t
                        pe.wait_ge(s.ya_out.sem, s.ya_out.f.next(pe))
                        product(pe, ps[:, 2 + i % 4, :],
                                lambda k: (ring.hi[w][:, k * WC + c * P:k * WC + (c + 1) * P],
                                           ring.lo[w][:, k * WC + c * P:k * WC + (c + 1) * P]),
                                lambda k: (ahi[:, k, t * NT:(t + 1) * NT], alo[:, k, t * NT:(t + 1) * NT]),
                                KA).then_inc(s.ya_done.sem, 1)
            pe.wait_ge(s.z_split.sem, s.z_split.d.next(pe, KD))
            for n in range(2, 6):
                pe.wait_ge(ring.ready[slot(n)].sem, ring.ready[slot(n)].d.next(pe))
                w = slot(n)
                for c in range(2):
                    for t in range(2):
                        i = ((n - 2) * 2 + c) * 2 + t
                        pe.wait_ge(s.y_out.sem, s.y_out.f.next(pe))
                        product(pe, ps[:, y_banks[i % 4], :],
                                lambda k: (ring.hi[w][:, k * SC + c * P:k * SC + (c + 1) * P],
                                           ring.lo[w][:, k * SC + c * P:k * SC + (c + 1) * P]),
                                lambda k: (zhi[:, k, t * NT:(t + 1) * NT], zlo[:, k, t * NT:(t + 1) * NT]),
                                KD).then_inc(s.y_done.sem, 1)
            pe.wait_ge(s.ya_out.sem, s.ya_out.drained(pe))
            s.post.sums(pe, env, ps, (2, 3), acc)
            pe.wait_ge(s.post.rooted.sem, s.post.rooted.d.next(pe))
            s.next.sums(pe, env, ps, (2, 3), acc)


def make_ffn_signals(env):
    s = Env()
    s.cleared = Signal(env, "f_cleared")
    s.taps = Signal(env, "f_taps")
    s.g_done, s.g_out = Signal(env, "f_g_done"), Signal(env, "f_g_out", 3)
    s.conv_step = Signal(env, "f_conv_step")
    s.conv_done = Signal(env, "f_conv_done")
    s.gelu_done = Signal(env, "f_gelu_done")
    s.a_done, s.a_out = Signal(env, "f_a_done"), Signal(env, "f_a_out", 2)
    s.m_rounded, s.m_ready = Signal(env, "f_m_rounded"), Signal(env, "f_m_ready")
    s.d_done, s.d_out = Signal(env, "f_d_done"), Signal(env, "f_d_out", 3)
    s.post = Norm(env, "f_post")
    s.x_in = [Signal(env, f"f_x_in{i}") for i in range(2)]
    s.y_scaled, s.x_sum = Signal(env, "f_y_scaled"), Signal(env, "f_x_sum")
    s.o_turned, s.o_out = Signal(env, "f_o_turned"), Signal(env, "f_o_out", 2)
    s.o_stored = [Signal(env, f"f_o_stored{i}", 16) for i in range(2)]
    return s


def ffn(nc, env, io, out, b):
    ring, hl, s = env.ring, env.hload, env.fsig
    t0 = b * BLK
    tag = f"f{b}"
    w_up, w_down = io["w_up"][0], io["w_down"][0]
    G, DN, A = 0, 1, 2
    with ExitStack() as ctx:
        sb = lambda n, sh, d=F32: ctx.enter_context(nc.sbuf_tensor(f"{n}_{tag}", sh, d))
        ring.tensors(nc, ctx, tag)
        hhi, hlo = sb("h_hi", [P, KD, HW], F32R), sb("h_lo", [P, KD, HW], F32R)
        y = sb("y", [P, KD, BLK])
        mhi, mlo = sb("m_hi", [P, 2, BLK], F32R), sb("m_lo", [P, 2, BLK], F32R)
        gx = sb("gx", [P, HW])
        cv = [sb(f"cv{i}", [P, BLK]) for i in range(2)]
        taps = sb("taps", [P, 4, 2])
        ps = ctx.enter_context(nc.psum_tensor(f"ps_{tag}", [P, 8, 512], F32))
        yf = y[:].rearrange("p k t -> p (k t)")
        raw = [yf[:, (i + 1) * HW:(i + 2) * HW] for i in range(4)]
        rbuf = yf[:, 0:HW]
        params = env.param[:, 108:196].rearrange("p (r c) -> p r c", c=FC)
        block = ctx.enter_context(nc.Block())

        def up(col):
            return bass.AP(tensor=w_up.tensor, offset=w_up.offset + col, ap=[[2 * D_FF, P], [P * 2 * D_FF, KD], [1, SC]])

        def down(word):
            return bass.AP(tensor=w_down.tensor, offset=w_down.offset + word, ap=[[D, P], [P * D, 2], [1, D]])

        def ostage(t):
            return ring.stage[t % 2][:, 0:D]

        @block.sync
        def _(sp):
            ring.load(sp, G, up(D_FF))
            hl.load(sp, b, env.x1_d, env.r2_d, rbuf, raw)
            ring.load(sp, A, up(0))
            ring.load(sp, DN, down(0))
            ring.load(sp, G, up(D_FF + SC))
            ring.load(sp, A, up(SC))
            with repeat(sp, FG - 2, ring.per((1, 1, 1), "load")) as i:
                row, g_col, a_col = (sp.snap(x) for x in ((i + 1) * (SC * D), (i + 2) * SC + D_FF, (i + 2) * SC))
                ring.load(sp, DN, down(row))
                ring.load(sp, G, up(g_col))
                ring.load(sp, A, up(a_col))
            ring.load(sp, DN, down((FG - 1) * SC * D))
            for k in range(KD):
                if k == 0:
                    sp.wait_ge(s.post.added.sem, s.post.added.d.next(sp, KD))
                if k >= 2:
                    sp.wait_ge(s.x_sum.sem, s.x_sum.d.next(sp))
                sp.dma_start(cv[k % 2][:], env.x1_d[k * P:(k + 1) * P, t0:t0 + BLK]).then_inc(s.x_in[k % 2].sem, 16)
            sp.wait_ge(s.x_sum.sem, s.x_sum.d.next(sp, 2))

        @block.gpsimd
        def _(pool):
            hl.edges(pool, b, hhi, hlo)
            pool.wait_ge(hl.ready.sem, hl.ready.d.next(pool, KD))
            pool.memset(y[:], 0.0).then_inc(s.cleared.sem, 1)
            pool.wait_ge(s.m_ready.sem, s.m_ready.d.next(pool, 2 * FG))
            for k in range(KD):
                s.post.add(pool, k, gx[:, 0:BLK], cv[k % 2])

        @block.scalar
        def _(act):
            ring.round(act, G)
            hl.scalar(act, b, env.scale2, env.shift2, raw, hhi)
            for x in (A, DN):
                ring.round(act, x)

            def g_part(i, more, first=False):
                act.activation(taps[:], params[:, :, bass.ds(i * 2, 2)], ACT.Copy).then_inc(s.taps.sem, 1)
                act.wait_ge(s.taps.sem, s.taps.d.next(act))
                for c in range(2):
                    if c == 1:
                        act.wait_ge(s.conv_done.sem, s.conv_done.d.next(act))
                    for t in range(3):
                        act.wait_ge(s.g_done.sem, s.g_done.d.next(act))
                        bank = 5 + t if first and c == 1 else t
                        cols = min(HT, BLK - t * HT)
                        act.activation(cv[c][:, t * HT:t * HT + cols], ps[:, bank, 0:cols], ACT.Copy,
                                       scale=taps[:, 0, c:c + 1]).then_inc(s.conv_step.sem, 1)
                        act.activation(gx[:, t * HT:(t + 1) * HT], ps[:, bank, 0:HT], ACT.Copy).then_inc(s.g_out.sem, 1)
                    if c == 1:
                        if more:
                            ring.round(act, G)
                        gelu(0)
                act.wait_ge(s.conv_done.sem, s.conv_done.d.next(act))
                gelu(1)

            def gelu(c):
                act.activation(cv[c][:], cv[c][:], ACT.Gelu_apprx_tanh, bias=taps[:, 3, c:c + 1]).then_inc(s.gelu_done.sem, 1)

            def d_part(more):
                act.wait_ge(s.d_done.sem, s.d_done.d.next(act, 16))
                if more:
                    ring.round(act, DN)

            def a_part(more):
                for c in range(2):
                    act.wait_ge(s.a_out.sem, s.a_out.d.next(act, 2))
                    act.activation(mhi[:, c, :], cv[c][:], ACT.Copy).then_inc(s.m_rounded.sem, 1)
                if more:
                    ring.round(act, A)
                act.wait_ge(s.m_ready.sem, s.m_ready.d.next(act, 2))

            g_part(0, True, True)
            a_part(True)
            with repeat(act, FG - 2, {
                    s.taps.d: 1, s.conv_done.d: 2, s.g_done.d: 6, s.d_done.d: 16, s.a_out.d: 4, s.m_ready.d: 2,
                    **ring.per((1, 1, 1), "round")}) as i:
                g_part(i + 1, True)
                d_part(True)
                a_part(True)
            g_part(FG - 1, False)
            d_part(True)
            a_part(False)
            d_part(False)
            for k in range(KD):
                act.wait_ge(s.post.added.sem, s.post.added.f.next(act))
                if k == 0:
                    act.wait_ge(s.d_out.sem, s.d_out.d.next(act, 16 * FG))
                act.activation(cv[k % 2][:], y[:, k, :], ACT.Square).then_inc(s.post.squared.sem, 1)
            s.post.root(act, env, ps, (0, 1), gx)
            for t in range(BLK // P):
                act.wait_ge(s.o_out.sem, s.o_out.d.next(act))
                act.dma_start(out[0, t0 + t * P:t0 + (t + 1) * P, :], ostage(t)).then_inc(s.o_stored[t % 2].sem, 16)
            for i in range(2):
                act.wait_ge(s.o_stored[i].sem, s.o_stored[i].d.next(act, 16 * BLK // P // 2))

        @block.vector
        def _(dve):
            ring.rest(dve, G)
            hl.vector(dve, b, rbuf, raw, hhi, hlo)
            for x in (A, DN):
                ring.rest(dve, x)

            def g_part():
                dve.wait_ge(s.taps.sem, s.taps.d.next(dve))
                for c in range(2):
                    dve.wait_ge(s.g_out.sem, s.g_out.d.next(dve, 3))
                    dve.wait_ge(s.conv_step.sem, s.conv_step.d.next(dve, 3))
                    dve.scalar_tensor_tensor(out=cv[c][:], in0=gx[:, 1:1 + BLK], scalar=taps[:, 1, c:c + 1],
                                             in1=cv[c][:], op0=ALU.mult, op1=ALU.add).then_inc(s.conv_step.sem, 1)
                    dve.wait_ge(s.conv_step.sem, s.conv_step.d.next(dve))
                    dve.scalar_tensor_tensor(out=cv[c][:], in0=gx[:, 2:2 + BLK], scalar=taps[:, 2, c:c + 1],
                                             in1=cv[c][:], op0=ALU.mult, op1=ALU.add).then_inc(s.conv_done.sem, 1)

            def d_part(more_g, more_d):
                for j in range(KD):
                    for t in range(2):
                        dve.wait_ge(s.d_done.sem, s.d_done.d.next(dve))
                        o = y[:, j, t * NT:(t + 1) * NT]
                        dve.tensor_tensor(o, ps[:, 5 + (2 * j + t) % 3, :], o, ALU.add).then_inc(s.d_out.sem, 1)
                    if more_g and j == 3:
                        ring.rest(dve, G)
                if more_d:
                    ring.rest(dve, DN)

            def a_part(more):
                for c in range(2):
                    dve.wait_ge(s.gelu_done.sem, s.gelu_done.d.next(dve))
                    for t in range(2):
                        dve.wait_ge(s.a_done.sem, s.a_done.d.next(dve))
                        o = cv[c][:, t * NT:(t + 1) * NT]
                        dve.tensor_tensor(o, ps[:, 3 + t, :], o, ALU.mult).then_inc(s.a_out.sem, 1)
                    dve.wait_ge(s.m_rounded.sem, s.m_rounded.d.next(dve))
                    dve.tensor_tensor(mlo[:, c, :], cv[c][:], mhi[:, c, :].bitcast(F32), ALU.subtract).then_inc(s.m_ready.sem, 1)
                if more:
                    ring.rest(dve, A)

            g_part()
            ring.rest(dve, G)
            a_part(True)
            dve.wait_ge(s.cleared.sem, s.cleared.d.next(dve))
            with repeat(dve, FG - 2, {
                    s.taps.d: 1, s.g_out.d: 6, s.conv_step.d: 8, s.d_done.d: 16, s.gelu_done.d: 2,
                    s.a_done.d: 4, s.m_rounded.d: 2, **ring.per((1, 1, 1), "rest")}):
                g_part()
                d_part(True, True)
                a_part(True)
            g_part()
            d_part(False, True)
            a_part(False)
            d_part(False, False)
            s.post.inverse(dve, gx[:, 0:BLK])
            dve.wait_ge(s.post.ready.sem, s.post.ready.d.next(dve))
            for k in range(KD):
                dve.wait_ge(s.x_in[k % 2].sem, s.x_in[k % 2].d.next(dve, 16))
                dve.scalar_tensor_tensor(out=y[:, k, :], in0=y[:, k, :], scalar=env.gate2[:, k:k + 1],
                                         in1=gx[:, 0:BLK], op0=ALU.mult, op1=ALU.mult).then_inc(s.y_scaled.sem, 1)
                dve.wait_ge(s.y_scaled.sem, s.y_scaled.d.next(dve))
                dve.tensor_tensor(y[:, k, :], y[:, k, :], cv[k % 2][:], ALU.add).then_inc(s.x_sum.sem, 1)
            for t in range(BLK // P):
                dve.wait_ge(s.o_stored[t % 2].sem, s.o_stored[t % 2].f.next(dve, 16))
                dve.wait_ge(s.o_turned.sem, s.o_turned.d.next(dve))
                dve.tensor_copy(ostage(t), ps[:, 4 * (t % 2):4 * (t % 2) + 2, :].rearrange("p a b -> p (a b)")).then_inc(s.o_out.sem, 1)

        @block.tensor
        def _(pe):
            chunk_wait = hl.chunk_wait(pe, b)

            def up_tiles(x, done, free, bank, tiles, a0, cols):
                pe.wait_ge(ring.ready[x].sem, ring.ready[x].d.next(pe))
                for c in range(2):
                    for t in range(tiles):
                        pe.wait_ge(free.sem, free.f.next(pe))
                        a = slice(a0 + t * cols, a0 + (t + 1) * cols)
                        product(pe, ps[:, bank + t, 0:cols],
                                lambda k: (ring.hi[x][:, k * SC + c * P:k * SC + (c + 1) * P],
                                           ring.lo[x][:, k * SC + c * P:k * SC + (c + 1) * P]),
                                lambda k: (hhi[:, k, a], hlo[:, k, a]),
                                KD).then_inc(done.sem, 1)

            def first_tile(c, t):
                a = slice(t * HT, (t + 1) * HT)
                return (ps[:, 5 * c + t, 0:HT],
                        lambda k: (ring.hi[G][:, k * SC + c * P:k * SC + (c + 1) * P],
                                   ring.lo[G][:, k * SC + c * P:k * SC + (c + 1) * P]),
                        lambda k: (hhi[:, k, a], hlo[:, k, a]), s.g_done)

            def g_part():
                up_tiles(G, s.g_done, s.g_out, 0, 3, 0, HT)

            def a_part():
                up_tiles(A, s.a_done, s.a_out, 3, 2, 1, NT)

            def d_part():
                pe.wait_ge(ring.ready[DN].sem, ring.ready[DN].d.next(pe))
                pe.wait_ge(s.m_ready.sem, s.m_ready.d.next(pe, 2))
                for j in range(KD):
                    for t in range(2):
                        pe.wait_ge(s.d_out.sem, s.d_out.f.next(pe))
                        product(pe, ps[:, 5 + (2 * j + t) % 3, :],
                                lambda k: (ring.hi[DN][:, k * D + j * P:k * D + (j + 1) * P],
                                           ring.lo[DN][:, k * D + j * P:k * D + (j + 1) * P]),
                                lambda k: (mhi[:, k, t * NT:(t + 1) * NT], mlo[:, k, t * NT:(t + 1) * NT]),
                                2).then_inc(s.d_done.sem, 1)

            pe.wait_ge(ring.ready[G].sem, ring.ready[G].d.next(pe))
            s.g_out.f.skip(pe, 6)
            products_together(pe, [first_tile(c, t) for c in range(2) for t in range(3)], KD, chunk_wait)
            a_part()
            with repeat(pe, FG - 1, {
                    s.g_out.f: 6, s.a_out.f: 4, s.m_ready.d: 2, s.d_out.f: 16, **ring.per((1, 1, 1), "use")}):
                g_part()
                d_part()
                a_part()
            d_part()
            pe.wait_ge(s.g_out.sem, s.g_out.drained(pe))
            s.post.sums(pe, env, ps, (0, 1), gx)
            pe.wait_ge(s.x_sum.sem, s.x_sum.d.next(pe, KD))
            for t in range(BLK // P):
                pe.wait_ge(s.o_out.sem, s.o_out.f.next(pe))
                for k in range(KD):
                    bank = 4 * (t % 2) + k // 4
                    last = pe.transpose(ps[:, bank, (k % 4) * P:(k % 4 + 1) * P], y[:, k, t * P:(t + 1) * P], env.ident[:])
                last.then_inc(s.o_turned.sem, 1)


def build(nc, io, out):
    env = Env()
    env.nc = nc
    env.credits, env.signals = [], []
    with ExitStack() as stack:
        env.stack = stack
        dram = lambda n, s: nc.dram_tensor(n, s, F32).ap()
        env.xt_d = dram("xt_d", [D, NTOK])
        env.r_d = dram("r_d", [NTOK])
        env.qk_d = dram("qk_d", [2 * ATT_W, NTOK])
        env.v_d = dram("v_d", [NTOK, ATT_W])
        env.ga_d = dram("ga_d", [D, SEQ])
        env.cb_d = dram("cb_d", [D, SEQ])
        env.att_d = dram("att_d", [SEQ, ATT_W])
        env.x1_d = dram("x1_d", [D, SEQ])
        env.r2_d = dram("r2_d", [SEQ])
        env.pad_d = dram("pad_d", [HEADS, 17, P])
        env.bt_d = dram("bt_d", [HEADS, P, TCOLS])
        sb = lambda n, s: stack.enter_context(nc.sbuf_tensor(n, s, F32))
        env.ident, env.ones, env.eps = sb("ident", [P, P]), sb("ones", [P, P]), sb("eps", [P, 1])
        env.param = sb("param", [P, 196])
        env.shift1, env.scale1, env.gate1 = sb("shift1", [P, KD]), sb("scale1", [P, KD]), sb("gate1", [P, KD])
        env.shift2, env.scale2, env.gate2 = sb("shift2", [P, KD]), sb("scale2", [P, KD]), sb("gate2", [P, KD])
        env.shiftc, env.scalec = sb("shiftc", [P, KD]), sb("scalec", [P, KD])
        env.ring, env.hload = Ring(env), HLoad(env)
        env.psig = make_projection_signals(env)
        env.pad_dma, env.tab_in, env.tab_stored = (Signal(env, n) for n in ("pad_dma", "tab_in", "tab_stored"))
        with ExitStack() as own:
            env.stack, env.signals = own, []
            setup(nc, env, io)
            with nc.Block() as block:
                @block.gpsimd
                def _(pool):
                    for s in env.signals:
                        pool.sem_clear(s.sem)
        env.stack = stack
        env.asig = make_attention_signals(env)
        env.msig, env.fsig = make_merge_signals(env), make_ffn_signals(env)
        with nc.Block() as block:
            @block.gpsimd
            def _(pool):
                for s in env.credits:
                    pool.sem_inc(s.sem, s.credit)
        for b in (None, 0, 1):
            projections(nc, env, io, b)
        attention(nc, env)
        for b in range(NB):
            merge(nc, env, io, b)
        for b in range(NB):
            ffn(nc, env, io, out, b)


_INS = ["x", "c", "ctx", "c_ctx", "w_ada", "b_ada", "g_pre_mix", "g_post_mix", "g_pre_ffn", "g_post_ffn",
        "w_in", "rpb", "w_short_conv", "w_branch_attn", "w_branch_conv", "w_out",
        "w_up", "w_ffn_conv", "b_ffn_conv", "w_down"]


def kernel(**inputs):
    import concourse.bacc as bacc
    from concourse.bass_utils import run_bass_kernel_spmd

    nc = bacc.Bacc("TRN2", target_bir_lowering=False, num_devices=1)
    arrays, io = {}, {}
    for name in _INS:
        a = np.ascontiguousarray(inputs[name])
        arrays[f"in_{name}"] = a
        io[name] = nc.dram_tensor(f"in_{name}", a.shape, mybir.dt.from_np(a.dtype), kind="ExternalInput").ap()
    out = nc.dram_tensor("out_0", (1, SEQ, D), F32, kind="ExternalOutput").ap()
    build(nc, io, out)
    r = run_bass_kernel_spmd(nc, [arrays], core_ids=[0])
    return r.results[0]["out_0"]
```

```python
from contextlib import ExitStack, contextmanager

import numpy as np

import concourse.bass as bass
from concourse import mybir

ALU = mybir.AluOpType
ACT = mybir.ActivationFunctionType
AX = mybir.AxisListType
F32 = mybir.dt.float32
F32R = mybir.dt.float32r
I32 = mybir.dt.int32

P = 128
D = 1024
SEQ = 2048
CTX = 256
NTOK = SEQ + CTX
GRID_W = 64
HEADS = 8
DH = 64
ATT_W = HEADS * DH
CONV_W = 512
D_FF = 2816
WIN_H = 8
WIN_W = 16
EPS = 1e-6
NEG = -1e30
IN_W = 3 * ATT_W + 3 * CONV_W + 2 * D

KD = D // P
KA = ATT_W // P
BLK = 1024
NB = SEQ // BLK
HW = BLK + 2
HT = HW // 3
NT = 512
SC = 256
SLAB = KD * SC
RING = 3
FG = D_FF // SC
FC = D_FF // P
TT = SEQ // P
ROWS = SEQ // GRID_W
PAIRS = ROWS // 2
TROWS = 16
WROWS = 10
WIN = WROWS * GRID_W
TCOLS = TROWS * GRID_W + WIN


class Tally:

    def __init__(self, sem, credit):
        self.sem, self.credit = sem, credit
        self.seen = {}
        self.loops = {}

    def value(self, eng):
        i, per = self.loops.get(eng.engine, (None, 0))
        n = self.seen.get(eng.engine, 0) + self.credit
        return n if i is None else n + i * per

    def next(self, eng, k=1):
        self.seen[eng.engine] = self.seen.get(eng.engine, 0) + k
        return self.value(eng)

    def skip(self, eng, k):
        self.seen[eng.engine] = self.seen.get(eng.engine, 0) + k


class Signal:

    def __init__(self, env, name, credit=0):
        self.sem = env.stack.enter_context(env.nc.semaphore(name))
        self.credit = credit
        self.d = Tally(self.sem, credit)
        self.f = Tally(self.sem, 0)
        env.signals.append(self)
        if credit:
            env.credits.append(self)

    def drained(self, eng):
        return self.f.value(eng) + self.credit


@contextmanager
def repeat(eng, trips, per):
    e = eng.engine
    before = {t: t.seen.get(e, 0) for t in per}
    with eng.Fori(0, trips) as i:
        for t, n in per.items():
            t.loops[e] = (i, n)
        yield i
    for t, n in per.items():
        assert t.seen.get(e, 0) - before[t] == n, (t.sem, t.seen.get(e, 0) - before[t], n)
        t.seen[e] = before[t] + n * trips
        del t.loops[e]


class Env:
    pass


def slab(w, kc, col, cols):
    n = w.shape[-1]
    return bass.AP(tensor=w.tensor, offset=w.offset + col, ap=[[n, P], [P * n, kc], [1, cols]])


def product(pe, out, w, a, kc):
    for k in range(kc):
        w0, w1 = w(k)
        a0, a1 = a(k)
        pe.matmul(out, w0, a0, start=(k == 0), stop=False)
        pe.matmul(out, w0, a1, start=False, stop=False)
        last = pe.matmul(out, w1, a0, start=False, stop=(k == kc - 1))
    return last


def products_together(pe, tiles, kc, chunk_wait):
    for k in range(kc):
        chunk_wait(k)
        for out, w, a, done in tiles:
            w0, w1 = w(k)
            a0, a1 = a(k)
            pe.matmul(out, w0, a0, start=(k == 0), stop=False)
            pe.matmul(out, w0, a1, start=False, stop=False)
            last = pe.matmul(out, w1, a0, start=False, stop=(k == kc - 1))
            if k == kc - 1:
                last.then_inc(done.sem, 1)


def setup(nc, env, io):
    with ExitStack() as ctx:
        sb = lambda n, s, d=F32: ctx.enter_context(nc.sbuf_tensor(n, s, d))
        sig = lambda n: Signal(env, n)
        rows1 = sb("rows1", [108, P])
        rows2 = sb("rows2", [88, P])
        csig = sb("csig", [P, 16])
        csil = env.csil
        aw = sb("aw", [P, 4, SLAB])
        xr = sb("xr", [P, 3, D])
        sq = sb("sq", [P, D])
        xts = sb("xts", [P, 2, KD, NT])
        ss = sb("ss", [P, 18])
        rt = sb("rt", [P, 18])
        rr = sb("rr", [P, 18])
        rrow = sb("rrow", [18, P])
        modt = sb("modt", [P, 16])
        modc = sb("modc", [P, 16])
        zero = sb("zero", [P, 136])
        valid = sb("valid", [64, GRID_W])
        cut = sb("cut", [P, GRID_W], I32)
        neg = sb("neg", [P, GRID_W])
        bias_in = sb("bias_in", [HEADS * 15, 31])
        bias_rev = sb("bias_rev", [HEADS * 15, 31])
        tab_rev = [sb(f"tab_rev{i}", [P, TROWS, GRID_W]) for i in range(2)]
        tab = [sb(f"tab{i}", [P, TROWS, GRID_W]) for i in range(2)]
        tabi = [sb(f"tabi{i}", [P, WROWS, GRID_W]) for i in range(2)]
        ps_x = ctx.enter_context(nc.psum_tensor("ps_x", [P, 2, KD, P], F32))
        ps_m = ctx.enter_context(nc.psum_tensor("ps_m", [P, 32], F32))
        ps_p = ctx.enter_context(nc.psum_tensor("ps_p", [P, 512], F32))

        rows_in = sig("rows_in")
        const_set = sig("const_set")
        params_turned = sig("params_turned")
        params_out = sig("params_out")
        c_sigmoid = sig("c_sigmoid")
        c_silu = sig("c_silu")
        ada_in = [sig(f"ada_in{s}") for s in range(4)]
        ada_used = sig("ada_used")
        mod_step = sig("mod_step")
        x_in = [sig(f"x_in{s}") for s in range(3)]
        x_squared = sig("x_squared")
        x_turned = sig("x_turned")
        x_evicted = sig("x_evicted")
        xt_stored = [sig(f"xt_stored{i}") for i in range(2)]
        root = sig("root")
        inverse = sig("inverse")
        r_turned = sig("r_turned")
        r_out = sig("r_out")
        r_stored = sig("r_stored")
        pad_dma = env.pad_dma
        cut_set = sig("cut_set")
        bias_loaded, bias_turned, tab_turned = sig("bias_loaded"), sig("bias_turned"), sig("tab_turned")
        tab_in = env.tab_in
        tab_cut = sig("tab_cut")
        tab_inner = sig("tab_inner")
        tab_stored = env.tab_stored

        n_ada = 2 * D // SC
        toks = TT + CTX // P
        xsrc = [io["x"][0, t * P:(t + 1) * P, :] if t < TT else io["ctx"][0, (t - TT) * P:(t - TT + 1) * P, :]
                for t in range(toks)]
        param = env.param
        row_view = lambda a, n: a.rearrange("(r c) -> r c", c=P)

        block = ctx.enter_context(nc.Block())

        @block.sync
        def _(sp):
            sp.dma_start(bias_in[:], io["rpb"][0].rearrange("h r c -> (h r) c")).then_inc(bias_loaded.sem, 16)
            r = 0
            for a in (io["b_ada"][0], io["g_pre_mix"][0], io["g_post_mix"][0], io["g_pre_ffn"][0],
                      io["g_post_ffn"][0], io["c"][0], io["c_ctx"],
                      io["w_short_conv"][0].rearrange("t c -> (t c)")):
                n = a.shape[0] // P
                sp.dma_start(rows1[r:r + n, :], row_view(a, n)).then_inc(rows_in.sem, 16)
                r += n
            sp.dma_start(rows2[0:66, :], row_view(io["w_ffn_conv"][0].rearrange("t c -> (t c)"), 66)).then_inc(rows_in.sem, 16)
            sp.dma_start(rows2[66:88, :], row_view(io["b_ffn_conv"][0], 22)).then_inc(rows_in.sem, 16)
            for n in range(max(n_ada, toks)):
                if n < toks:
                    if n >= 3:
                        sp.wait_ge(x_turned.sem, x_turned.d.next(sp))
                        sp.wait_ge(x_squared.sem, x_squared.d.next(sp))
                    sp.dma_start(xr[:, n % 3, :], xsrc[n]).then_inc(x_in[n % 3].sem, 16)
                if n < n_ada:
                    if n >= 4:
                        sp.wait_ge(ada_used.sem, ada_used.d.next(sp))
                    sp.dma_start(aw[:, n % 4, :].rearrange("p (k c) -> p k c", k=KD),
                                 slab(io["w_ada"][0], KD, n * SC, SC)).then_inc(ada_in[n % 4].sem, 16)
            sp.wait_ge(r_out.sem, r_out.d.next(sp))
            sp.dma_start(env.r_d[0:NTOK].rearrange("(t p) -> t p", p=P), rrow[:]).then_inc(r_stored.sem, 16)
            sp.wait_ge(r_stored.sem, r_stored.d.next(sp, 16))

        @block.gpsimd
        def _(pool):
            pool.memset(env.ident[:], 1.0).then_inc(const_set.sem, 1)
            pool.memset(env.ones[:], 1.0).then_inc(const_set.sem, 1)
            pool.memset(env.eps[:], EPS).then_inc(const_set.sem, 1)
            pool.memset(zero[:], 0.0).then_inc(const_set.sem, 1)
            pool.memset(valid[:], 1.0).then_inc(const_set.sem, 1)
            pool.memset(neg[:], NEG).then_inc(const_set.sem, 1)
            pool.wait_ge(const_set.sem, const_set.d.next(pool, 6))
            pool.affine_select(out=env.ident[:], in_=env.ident[:], compare_op=ALU.is_equal, fill=0.0, base=0,
                               pattern=[[-1, P]], channel_multiplier=1).then_inc(const_set.sem, 1)
            c0 = GRID_W - WIN_W
            pool.affine_select(out=valid[:, 0:c0], in_=valid[:, 0:c0], compare_op=ALU.is_ge, fill=0.0,
                               base=WIN_W // 2, pattern=[[1, c0]], channel_multiplier=-1).then_inc(const_set.sem, 1)
            pool.wait_ge(const_set.sem, const_set.d.next(pool, 2))
            pool.affine_select(out=valid[:, WIN_W:GRID_W], in_=valid[:, WIN_W:GRID_W], compare_op=ALU.is_ge,
                               fill=0.0, base=WIN_W // 2 - 1 - WIN_W, pattern=[[-1, c0]],
                               channel_multiplier=1).then_inc(const_set.sem, 1)
            pool.dma_start(env.pad_d.rearrange("h r c -> (h r c)").rearrange("(p f) -> p f", p=P),
                           zero[:]).then_inc(pad_dma.sem, 16)
            pool.wait_ge(pad_dma.sem, pad_dma.d.next(pool, 16))
            pool.wait_ge(bias_turned.sem, bias_turned.d.next(pool))
            for h in range(HEADS):
                pool.dma_start(env.pad_d[h, 1:16, 48:79], bias_rev[h * 15:(h + 1) * 15, :]).then_inc(pad_dma.sem, 16)
            pool.wait_ge(cut_set.sem, cut_set.d.next(pool))
            pool.dma_start(cut[64:128, :], cut[0:64, :]).then_inc(pad_dma.sem, 16)
            pool.wait_ge(pad_dma.sem, pad_dma.d.next(pool, 16 * (HEADS + 1)))

            def load_table(h):
                for half in range(2):
                    pool.dma_start(tab_rev[h % 2][64 * half:64 * half + 64, :, :],
                                   bass.AP(tensor=env.pad_d.tensor, offset=h * 17 * P + (1 - half) * P,
                                           ap=[[1, 64], [P, TROWS], [1, GRID_W]])).then_inc(tab_in[h % 2].sem, 16)

            load_table(0)
            for h in range(HEADS):
                stored = tab_stored[h % 2]
                if h + 1 < HEADS:
                    load_table(h + 1)
                pool.wait_ge(tab_cut.sem, tab_cut.d.next(pool))
                if h >= 2:
                    pool.wait_ge(stored.sem, stored.d.next(pool, 32))
                pool.dma_start(env.bt_d[h, :, 0:TROWS * GRID_W],
                               tab[h % 2][:].rearrange("p a b -> p (a b)")).then_inc(stored.sem, 16)
                inner = tabi[h % 2]
                pool.tensor_copy(inner[:], tab[h % 2][:, 3:3 + WROWS, :]).then_inc(tab_inner.sem, 1)
                pool.wait_ge(tab_inner.sem, tab_inner.d.next(pool))
                pool.memset(inner[0:64, 8:10, :], NEG).then_inc(tab_inner.sem, 1)
                pool.memset(inner[64:128, 9:10, :], NEG).then_inc(tab_inner.sem, 1)
                pool.memset(inner[64:128, 0:1, :], NEG).then_inc(tab_inner.sem, 1)
                pool.wait_ge(tab_inner.sem, tab_inner.d.next(pool, 3))
                pool.dma_start(env.bt_d[h, :, TROWS * GRID_W:TCOLS],
                               inner[:].rearrange("p a b -> p (a b)")).then_inc(stored.sem, 16)
            for x in tab_stored:
                pool.wait_ge(x.sem, x.d.next(pool, 32))

        @block.vector
        def _(dve):
            dve.wait_ge(const_set.sem, const_set.d.next(dve, 9))
            dve.tensor_scalar(cut[0:64, :], valid[:], 0.0, None, ALU.is_equal).then_inc(cut_set.sem, 1)
            dve.wait_ge(bias_loaded.sem, bias_loaded.d.next(dve, 16))
            dve.tensor_copy(bias_rev[:], bass.AP(tensor=bias_in[:].tensor, offset=bias_in[:].offset + 30,
                                                 ap=[[31, HEADS * 15], [-1, 31]])).then_inc(bias_turned.sem, 1)
            dve.wait_ge(params_turned.sem, params_turned.d.next(dve))
            dve.tensor_copy(param[:, 0:108], ps_p[:, 0:108]).then_inc(params_out.sem, 1)
            dve.tensor_copy(param[:, 108:196], ps_p[:, 108:196]).then_inc(params_out.sem, 1)
            dve.wait_ge(c_sigmoid.sem, c_sigmoid.d.next(dve))
            dve.wait_ge(params_out.sem, params_out.d.next(dve, 2))
            dve.tensor_tensor(csil[:], csig[:], param[:, 80:96], ALU.mult).then_inc(c_silu.sem, 1)
            dve.wait_ge(pad_dma.sem, pad_dma.d.next(dve, 16 * (HEADS + 2)))

            def turn(t):
                dve.wait_ge(x_turned.sem, x_turned.d.next(dve))
                if t % 4 == 0 and t >= 8:
                    dve.wait_ge(xt_stored[(t // 4) % 2].sem, xt_stored[(t // 4) % 2].d.next(dve, 16))
                dve.tensor_copy(xts[:, (t // 4) % 2, :, (t % 4) * P:(t % 4 + 1) * P],
                                ps_x[:, t % 2, :, :]).then_inc(x_evicted.sem, 1)

            def table(h):
                x, rev, stored = tab[h % 2], tab_rev[h % 2], tab_stored[h % 2]
                dve.wait_ge(tab_in[h % 2].sem, tab_in[h % 2].d.next(dve, 32))
                if h >= 2:
                    dve.wait_ge(stored.sem, stored.d.next(dve, 32))
                back = bass.AP(tensor=rev[:].tensor, offset=rev[:].offset + GRID_W - 1,
                               ap=[[TROWS * GRID_W, P], [GRID_W, TROWS], [-1, GRID_W]])
                dve.tensor_copy(x[:], back).then_inc(tab_turned.sem, 1)
                dve.wait_ge(tab_turned.sem, tab_turned.d.next(dve))
                dve.copy_predicated(x[:], cut[:].unsqueeze(1).broadcast_to([P, TROWS, GRID_W]),
                                    neg[:].unsqueeze(1).broadcast_to([P, TROWS, GRID_W])).then_inc(tab_cut.sem, 1)

            for t in range(toks):
                turn(t)
                if t % 2 == 1 and t // 2 < HEADS:
                    table(t // 2)
            dve.wait_ge(root.sem, root.d.next(dve))
            dve.reciprocal(rr[:], rt[:]).then_inc(inverse.sem, 1)
            dve.wait_ge(r_turned.sem, r_turned.d.next(dve))
            dve.tensor_copy(rrow[:], ps_p[0:18, 256:384]).then_inc(r_out.sem, 1)
            dve.wait_ge(ada_used.sem, ada_used.d.next(dve, n_ada))
            mv = ps_m[:].rearrange("p (m s) -> p s m", s=2)
            dve.tensor_tensor(modt[:], mv[:, 0, :], param[:, 0:16], ALU.add).then_inc(mod_step.sem, 1)
            dve.tensor_tensor(modc[:], mv[:, 1, :], param[:, 0:16], ALU.add).then_inc(mod_step.sem, 1)
            dve.wait_ge(mod_step.sem, mod_step.d.next(dve, 2))
            dve.tensor_copy(env.shift1[:], modt[:, 0:8])
            dve.scalar_tensor_tensor(out=env.scale1[:], in0=modt[:, 8:16], scalar=1.0, in1=param[:, 48:56],
                                     op0=ALU.add, op1=ALU.mult)
            dve.tensor_copy(env.shiftc[:], modc[:, 0:8])
            dve.scalar_tensor_tensor(out=env.scalec[:], in0=modc[:, 8:16], scalar=1.0, in1=param[:, 48:56],
                                     op0=ALU.add, op1=ALU.mult).then_inc(mod_step.sem, 1)

        @block.scalar
        def _(act):
            act.wait_ge(params_out.sem, params_out.d.next(act, 2))
            act.activation(csig[:], param[:, 80:96], ACT.Sigmoid).then_inc(c_sigmoid.sem, 1)
            for t in range(toks):
                act.wait_ge(x_in[t % 3].sem, x_in[t % 3].d.next(act, 16))
                if t >= 1:
                    act.wait_ge(x_squared.sem, x_squared.d.next(act))
                act.activation(sq[:], xr[:, t % 3, :], ACT.Square, accum_out=ss[:, t:t + 1]).then_inc(x_squared.sem, 1)
                if t % 4 == 3 or t == toks - 1:
                    g = t // 4
                    cols = (t % 4 + 1) * P
                    act.wait_ge(x_evicted.sem, x_evicted.d.next(act, t % 4 + 1))
                    act.dma_start(env.xt_d.rearrange("(k p) t -> p k t", p=P)[:, :, g * NT:g * NT + cols],
                                  xts[:, g % 2, :, 0:cols]).then_inc(xt_stored[g % 2].sem, 16)
            act.wait_ge(x_squared.sem, x_squared.d.next(act))
            act.wait_ge(const_set.sem, const_set.d.next(act, 9))
            act.activation(rt[:], ss[:], ACT.Sqrt, scale=1.0 / D, bias=env.eps[:, 0:1]).then_inc(root.sem, 1)
            act.wait_ge(xt_stored[0].sem, xt_stored[0].d.next(act, 16 * 3))
            act.wait_ge(xt_stored[1].sem, xt_stored[1].d.next(act, 16 * 2))

        @block.tensor
        def _(pe):
            pe.wait_ge(const_set.sem, const_set.d.next(pe, 9))
            pe.wait_ge(rows_in.sem, rows_in.d.next(pe, 16 * 10))
            pe.transpose(ps_p[:, 0:108], rows1[:], env.ident[0:108, 0:108])
            pe.transpose(ps_p[:, 108:196], rows2[:], env.ident[0:88, 0:88]).then_inc(params_turned.sem, 1)

            def turn(t):
                pe.wait_ge(x_in[t % 3].sem, x_in[t % 3].d.next(pe, 16))
                if t >= 2:
                    pe.wait_ge(x_evicted.sem, x_evicted.d.next(pe))
                for k in range(KD):
                    last = pe.transpose(ps_x[:, t % 2, k, :], xr[:, t % 3, k * P:(k + 1) * P], env.ident[:])
                last.then_inc(x_turned.sem, 1)

            cs = csil[:].rearrange("p (s k) -> p k s", s=2)

            def ada(n):
                pe.wait_ge(ada_in[n % 4].sem, ada_in[n % 4].d.next(pe, 16))
                w = aw[:, n % 4, :].rearrange("p (k c) -> p k c", k=KD)
                for c in range(SC // P):
                    m = n * (SC // P) + c
                    for k in range(KD):
                        last = pe.matmul(ps_m[:, 2 * m:2 * m + 2], w[:, k, c * P:(c + 1) * P], cs[:, k, :],
                                         start=(k == 0), stop=(k == KD - 1))
                last.then_inc(ada_used.sem, 1)

            for n in range(max(n_ada, toks)):
                if n < toks:
                    turn(n)
                if n == 0:
                    pe.wait_ge(c_silu.sem, c_silu.d.next(pe))
                if n < n_ada:
                    ada(n)
            pe.wait_ge(inverse.sem, inverse.d.next(pe))
            pe.transpose(ps_p[0:18, 256:384], rr[:], env.ident[:]).then_inc(r_turned.sem, 1)



class Ring:

    def __init__(self, env):
        self.loaded = [Signal(env, f"w_loaded{s}") for s in range(RING)]
        self.rounded = [Signal(env, f"w_rounded{s}") for s in range(RING)]
        self.asked = Signal(env, "w_asked")
        self.ready = [Signal(env, f"w_ready{s}", 1) for s in range(RING)]

    def tensors(self, nc, ctx, tag):
        sb = lambda n, d: [ctx.enter_context(nc.sbuf_tensor(f"{n}{s}_{tag}", [P, SLAB], d)) for s in range(RING)]
        self.stage, self.hi, self.lo = sb("w_stage", F32), sb("w_hi", F32R), sb("w_lo", F32R)

    def load(self, sp, s, src):
        kc, cols = src.shape[1], src.shape[2]
        sp.wait_ge(self.ready[s].sem, self.ready[s].f.next(sp))
        sp.sem_inc(self.asked.sem, 1)
        sp.dma_start(self.stage[s][:, 0:kc * cols].rearrange("p (k c) -> p k c", k=kc),
                     src).then_inc(self.loaded[s].sem, 16)

    def round(self, act, s, words=SLAB):
        act.wait_ge(self.loaded[s].sem, self.loaded[s].d.next(act, 16))
        act.activation(self.hi[s][:, 0:words], self.stage[s][:, 0:words], ACT.Copy).then_inc(self.rounded[s].sem, 1)

    def rest(self, dve, s, words=SLAB):
        dve.wait_ge(self.rounded[s].sem, self.rounded[s].d.next(dve))
        dve.tensor_tensor(self.lo[s][:, 0:words], self.stage[s][:, 0:words],
                          self.hi[s][:, 0:words].bitcast(F32), ALU.subtract).then_inc(self.ready[s].sem, 1)

    def per(self, counts, what):
        out = {}
        for s, n in enumerate(counts):
            out.update({"load": {self.ready[s].f: n},
                        "round": {self.loaded[s].d: 16 * n},
                        "rest": {self.rounded[s].d: n},
                        "use": {self.ready[s].d: n}}[what])
        return out


class HLoad:

    def __init__(self, env):
        self.r_in = Signal(env, "h_r_in")
        self.x_in = [Signal(env, f"h_x_in{s}") for s in range(4)]
        self.normed = Signal(env, "h_normed")
        self.modulated = Signal(env, "h_modulated")
        self.rounded = Signal(env, "h_rounded")
        self.ready = Signal(env, "h_ready")
        self.edge = Signal(env, "h_edge")

    def plan(self, b):
        if b is None:
            return SEQ, CTX, 0
        return (0, BLK + 1, 1) if b == 0 else (b * BLK - 1, BLK + 1, 0)

    def load(self, sp, b, src, rsrc, rbuf, xbuf, first_slab):
        t0, n, c0 = self.plan(b)
        sp.dma_start(rbuf[:, 0:n], rsrc[t0:t0 + n].partition_broadcast(P)).then_inc(self.r_in.sem, 16)
        for k in range(KD):
            if k >= 4:
                sp.wait_ge(self.ready.sem, self.ready.d.next(sp))
            sp.dma_start(xbuf[k % 4][:, 0:n], src[k * P:(k + 1) * P, t0:t0 + n]).then_inc(self.x_in[k % 4].sem, 16)
            if k == 0:
                first_slab()
        self.ready.d.skip(sp, 4)

    def vector(self, dve, b, rbuf, xbuf, hhi, hlo, first_slab):
        t0, n, c0 = self.plan(b)

        def rest(k):
            dve.wait_ge(self.rounded.sem, self.rounded.d.next(dve))
            dve.tensor_tensor(hlo[:, k, c0:c0 + n], xbuf[k % 4][:, 0:n], hhi[:, k, c0:c0 + n].bitcast(F32),
                              ALU.subtract).then_inc(self.ready.sem, 1)

        dve.wait_ge(self.r_in.sem, self.r_in.d.next(dve, 16))
        for k in range(KD):
            dve.wait_ge(self.x_in[k % 4].sem, self.x_in[k % 4].d.next(dve, 16))
            dve.tensor_tensor(xbuf[k % 4][:, 0:n], xbuf[k % 4][:, 0:n], rbuf[:, 0:n],
                              ALU.mult).then_inc(self.normed.sem, 1)
            if k >= 1:
                rest(k - 1)
            if k == 1:
                first_slab()
        rest(KD - 1)

    def scalar(self, act, b, scale, shift, xbuf, hhi, first_slab):
        t0, n, c0 = self.plan(b)
        for k in range(KD):
            act.wait_ge(self.normed.sem, self.normed.d.next(act))
            act.activation(xbuf[k % 4][:, 0:n], xbuf[k % 4][:, 0:n], ACT.Identity, scale=scale[:, k:k + 1],
                           bias=shift[:, k:k + 1]).then_inc(self.modulated.sem, 1)
            act.wait_ge(self.modulated.sem, self.modulated.d.next(act))
            act.activation(hhi[:, k, c0:c0 + n], xbuf[k % 4][:, 0:n], ACT.Copy).then_inc(self.rounded.sem, 1)
            if k == 0:
                first_slab()

    def edges(self, pool, b, hhi, hlo):
        c = 0 if b == 0 else HW - 1
        pool.memset(hhi[:, :, c:c + 1].bitcast(F32), 0.0).then_inc(self.edge.sem, 1)
        pool.memset(hlo[:, :, c:c + 1].bitcast(F32), 0.0).then_inc(self.edge.sem, 1)

    def chunk_wait(self, pe, b):
        def wait(k):
            if k == 0 and b is not None:
                pe.wait_ge(self.edge.sem, self.edge.d.next(pe, 2))
            pe.wait_ge(self.ready.sem, self.ready.d.next(pe))
        return wait


def make_projection_signals(env):
    s = Env()
    s.qk_done, s.qk_out = Signal(env, "qk_done"), Signal(env, "qk_out", 4)
    s.v_done, s.v_out = Signal(env, "v_done"), Signal(env, "v_out", 4)
    s.o_stored = [Signal(env, f"o_stored{i}", 16) for i in range(2)]
    s.cg_done, s.cg_out = Signal(env, "cg_done"), Signal(env, "cg_out", 3)
    s.hv_done, s.hv_out = Signal(env, "hv_done"), Signal(env, "hv_out", 3)
    s.bg_done, s.bg_out = Signal(env, "bg_done"), Signal(env, "bg_out", 2)
    s.conv_step = Signal(env, "conv_step")
    s.u_rounded, s.u_ready = Signal(env, "u_rounded"), Signal(env, "u_ready")
    s.gb_done, s.gb_out = Signal(env, "gb_done"), Signal(env, "gb_out", 4)
    s.yb_done, s.yb_out = Signal(env, "yb_done"), Signal(env, "yb_out", 2)
    s.ga_done, s.ga_out = Signal(env, "ga_done"), Signal(env, "ga_out", 2)
    s.cb_stored = [Signal(env, f"cb_stored{i}", 16) for i in range(2)]
    return s


def projections(nc, env, io, b):
    ring, hl, s = env.ring, env.hload, env.psig
    n_tok = CTX if b is None else BLK
    t0 = SEQ if b is None else b * BLK
    c0 = 0 if b is None else 1
    tag = f"p{b}"
    w_in = io["w_in"][0]
    with ExitStack() as ctx:
        sb = lambda n, s, d=F32: ctx.enter_context(nc.sbuf_tensor(f"{n}_{tag}", s, d))
        ring.tensors(nc, ctx, tag)
        hhi = sb("h_hi", [P, KD, HW], F32R)
        hlo = sb("h_lo", [P, KD, HW], F32R)
        uhi = sb("u_hi", [P, KA, BLK], F32R)
        ulo = sb("u_lo", [P, KA, BLK], F32R)
        tmp = [sb(f"tmp{i}", [P, HW]) for i in range(4)]
        rbuf = sb("rbuf", [P, HW])
        ostage = [sb(f"ostage{i}", [P, BLK]) for i in range(2)]
        ps = ctx.enter_context(nc.psum_tensor(f"ps_{tag}", [P, 8, 512], F32))

        first = 0 if b is not None else 2
        slabs = [("qk", slab(w_in, KD, j * SC, SC)) for j in range(first, 4)]
        slabs += [("v", slab(w_in, KD, 2 * ATT_W + j * SC, SC)) for j in range(2)]
        n_qkv = len(slabs)
        if b is not None:
            bg, cg, hv = (3 * ATT_W + i * CONV_W for i in range(3))
            ga = 3 * ATT_W + 3 * CONV_W
            for j in range(CONV_W // SC):
                slabs += [("conv", slab(w_in, KD, col + j * SC, SC)) for col in (cg, hv, bg)]
            for j in range(D // SC):
                slabs += [("gate", slab(w_in, KD, ga + D + j * SC, SC)),
                          ("gate", slab(io["w_branch_conv"][0], KA, j * SC, SC)),
                          ("gate", slab(w_in, KD, ga + j * SC, SC))]
        words = [x.shape[1] * x.shape[2] for _, x in slabs]
        step = min(NT, n_tok)
        nts = n_tok // step
        slot = lambda n: n % RING
        wcols = lambda c, k: slice(k * SC + c * P, k * SC + (c + 1) * P)

        block = ctx.enter_context(nc.Block())

        @block.sync
        def _(sp):
            hl.load(sp, b, env.xt_d, env.r_d, rbuf, tmp, lambda: ring.load(sp, slot(0), slabs[0][1]))
            for n in range(1, len(slabs)):
                ring.load(sp, slot(n), slabs[n][1])

        @block.gpsimd
        def _(pool):
            if b is not None:
                hl.edges(pool, b, hhi, hlo)
            hl.ready.d.skip(pool, KD)

        @block.scalar
        def _(act):
            hl.scalar(act, b, env.scalec if b is None else env.scale1,
                      env.shiftc if b is None else env.shift1, tmp, hhi,
                      lambda: ring.round(act, slot(0), words[0]))
            for n in range(1, RING):
                ring.round(act, slot(n), words[n])
            for n in range(n_qkv):
                if slabs[n][0] == "qk":
                    for c in range(2):
                        act.wait_ge(s.o_stored[c].sem, s.o_stored[c].f.next(act, 16))
                        for t in range(nts):
                            act.wait_ge(s.qk_done.sem, s.qk_done.d.next(act))
                            bank = 2 * c + t if nts == 2 else 2 * (n % 2) + c
                            act.activation(ostage[c][:, t * step:(t + 1) * step], ps[:, bank, 0:step], ACT.Copy,
                                           scale=DH ** -0.5 if first + n < 2 else 1.0).then_inc(s.qk_out.sem, 1)
                        act.wait_ge(s.qk_out.sem, s.qk_out.d.next(act, nts))
                        row = (first + n) * SC + c * P
                        act.dma_start(env.qk_d[row:row + P, t0:t0 + n_tok],
                                      ostage[c][:, 0:n_tok]).then_inc(s.o_stored[c].sem, 16)
                else:
                    for c in range(n_tok // P):
                        act.wait_ge(s.o_stored[c % 2].sem, s.o_stored[c % 2].f.next(act, 16))
                        act.wait_ge(s.v_done.sem, s.v_done.d.next(act))
                        i = c + (n - n_qkv + 2) * (n_tok // P)
                        act.activation(ostage[c % 2][:, 0:SC], ps[:, 4 + i % 4, 0:SC],
                                       ACT.Copy).then_inc(s.v_out.sem, 1)
                        act.wait_ge(s.v_out.sem, s.v_out.d.next(act))
                        col = (n - n_qkv + 2) * SC
                        act.dma_start(env.v_d[t0 + c * P:t0 + (c + 1) * P, col:col + SC],
                                      ostage[c % 2][:, 0:SC]).then_inc(s.o_stored[c % 2].sem, 16)
                if n + RING < len(slabs):
                    ring.round(act, slot(n), words[n + RING])
            if b is None:
                for c in range(2):
                    act.wait_ge(s.o_stored[c].sem, s.o_stored[c].drained(act))
                return
            for j in range(2):
                n = n_qkv + 3 * j
                for c in range(2):
                    for t in range(3):
                        act.wait_ge(s.cg_done.sem, s.cg_done.d.next(act))
                        act.activation(tmp[c][:, t * HT:(t + 1) * HT], ps[:, t, 0:HT],
                                       ACT.Copy).then_inc(s.cg_out.sem, 1)
                ring.round(act, slot(n), words[n + RING])
                act.wait_ge(s.hv_done.sem, s.hv_done.d.next(act, 6))
                ring.round(act, slot(n + 1), words[n + 1 + RING])
                for c in range(2):
                    act.wait_ge(s.bg_out.sem, s.bg_out.d.next(act, 2))
                    act.activation(uhi[:, 2 * j + c, :], tmp[2 + c][:, 0:BLK], ACT.Copy).then_inc(s.u_rounded.sem, 1)
                ring.round(act, slot(n + 2), words[n + 2 + RING])
            n = n_qkv + 6

            def rows(a, i, c):
                return bass.AP(tensor=a.tensor, offset=(i * 2 + c) * (P * SEQ) + t0, ap=[[SEQ, P], [1, BLK]])

            def gates(i, last):
                for c in range(2):
                    for t in range(2):
                        act.wait_ge(s.gb_done.sem, s.gb_done.d.next(act))
                        act.activation(tmp[c][:, t * NT:(t + 1) * NT], ps[:, 2 * c + t, :],
                                       ACT.Sigmoid).then_inc(s.gb_out.sem, 1)
                if not last:
                    ring.round(act, slot(n), words[n])
                act.wait_ge(s.yb_done.sem, s.yb_done.d.next(act, 4))
                for c in range(2):
                    act.wait_ge(s.yb_out.sem, s.yb_out.d.next(act, 2))
                    act.dma_start(rows(env.cb_d, i, c), tmp[2 + c][:, 0:BLK]).then_inc(s.cb_stored[c].sem, 16)
                if not last:
                    ring.round(act, slot(n + 1), words[n + 1])
                for c in range(2):
                    act.wait_ge(s.o_stored[c].sem, s.o_stored[c].f.next(act, 16))
                    for t in range(2):
                        act.wait_ge(s.ga_done.sem, s.ga_done.d.next(act))
                        act.activation(ostage[c][:, t * NT:(t + 1) * NT], ps[:, 6 + t, :],
                                       ACT.Sigmoid).then_inc(s.ga_out.sem, 1)
                    act.wait_ge(s.ga_out.sem, s.ga_out.d.next(act, 2))
                    act.dma_start(rows(env.ga_d, i, c), ostage[c][:]).then_inc(s.o_stored[c].sem, 16)
                if not last:
                    ring.round(act, slot(n + 2), words[n + 2])

            with repeat(act, 3, {s.gb_done.d: 4, s.ga_done.d: 4, s.yb_done.d: 4, s.yb_out.d: 4, s.ga_out.d: 4,
                                 s.o_stored[0].f: 16, s.o_stored[1].f: 16,
                                 **ring.per((1, 1, 1), "round")}) as i:
                gates(i, False)
            gates(3, True)
            for c in range(2):
                act.wait_ge(s.o_stored[c].sem, s.o_stored[c].drained(act))
                act.wait_ge(s.cb_stored[c].sem, s.cb_stored[c].d.next(act, 16 * 4))

        @block.vector
        def _(dve):
            hl.vector(dve, b, rbuf, tmp, hhi, hlo, lambda: ring.rest(dve, slot(0), words[0]))
            for n in range(1, RING):
                ring.rest(dve, slot(n), words[n])
            for n in range(n_qkv):
                if n + RING < len(slabs):
                    ring.rest(dve, slot(n), words[n + RING])
            if b is None:
                return
            for j in range(2):
                n = n_qkv + 3 * j
                ring.rest(dve, slot(n), words[n + RING])
                for c in range(2):
                    x, y = tmp[c], tmp[2 + c]
                    for t in range(3):
                        dve.wait_ge(s.hv_done.sem, s.hv_done.d.next(dve))
                        dve.wait_ge(s.cg_out.sem, s.cg_out.d.next(dve))
                        dve.tensor_tensor(x[:, t * HT:(t + 1) * HT], ps[:, 3 + t, 0:HT],
                                          x[:, t * HT:(t + 1) * HT], ALU.mult).then_inc(s.hv_out.sem, 1)
                    dve.wait_ge(s.hv_out.sem, s.hv_out.d.next(dve, 3))
                    tap = lambda k: env.param[:, 96 + k * KA + 2 * j + c:97 + k * KA + 2 * j + c]
                    dve.tensor_scalar(y[:, 0:BLK], x[:, 0:BLK], tap(0), None, ALU.mult).then_inc(s.conv_step.sem, 1)
                    for k in (1, 2):
                        dve.wait_ge(s.conv_step.sem, s.conv_step.d.next(dve))
                        dve.scalar_tensor_tensor(out=y[:, 0:BLK], in0=x[:, k:k + BLK], scalar=tap(k),
                                                 in1=y[:, 0:BLK], op0=ALU.mult,
                                                 op1=ALU.add).then_inc(s.conv_step.sem, 1)
                    dve.wait_ge(s.conv_step.sem, s.conv_step.d.next(dve))
                ring.rest(dve, slot(n + 1), words[n + 1 + RING])
                for c in range(2):
                    y = tmp[2 + c]
                    for t in range(2):
                        dve.wait_ge(s.bg_done.sem, s.bg_done.d.next(dve))
                        dve.tensor_tensor(y[:, t * NT:(t + 1) * NT], ps[:, 6 + t, :], y[:, t * NT:(t + 1) * NT],
                                          ALU.mult).then_inc(s.bg_out.sem, 1)
                for c in range(2):
                    dve.wait_ge(s.u_rounded.sem, s.u_rounded.d.next(dve))
                    dve.tensor_tensor(ulo[:, 2 * j + c, :], tmp[2 + c][:, 0:BLK],
                                      uhi[:, 2 * j + c, :].bitcast(F32), ALU.subtract).then_inc(s.u_ready.sem, 1)
                ring.rest(dve, slot(n + 2), words[n + 2 + RING])
            n = n_qkv + 6

            def gates(last):
                if not last:
                    ring.rest(dve, slot(n), words[n])
                for c in range(2):
                    dve.wait_ge(s.cb_stored[c].sem, s.cb_stored[c].f.next(dve, 16))
                    for t in range(2):
                        dve.wait_ge(s.gb_out.sem, s.gb_out.d.next(dve))
                        dve.wait_ge(s.yb_done.sem, s.yb_done.d.next(dve))
                        dve.tensor_tensor(tmp[2 + c][:, t * NT:(t + 1) * NT], ps[:, 4 + t, :],
                                          tmp[c][:, t * NT:(t + 1) * NT], ALU.mult).then_inc(s.yb_out.sem, 1)
                if not last:
                    ring.rest(dve, slot(n + 1), words[n + 1])
                    ring.rest(dve, slot(n + 2), words[n + 2])

            with repeat(dve, 3, {s.gb_out.d: 4, s.yb_done.d: 4, s.cb_stored[0].f: 16, s.cb_stored[1].f: 16,
                                 **ring.per((1, 1, 1), "rest")}):
                gates(False)
            gates(True)

        @block.tensor
        def _(pe):
            chunk_wait = hl.chunk_wait(pe, b)

            def channel_tile(n, c, bank, a0, cols, kc, ahi, alo, done):
                w = slot(n)
                product(pe, ps[:, bank, 0:cols],
                        lambda k: (ring.hi[w][:, wcols(c, k)], ring.lo[w][:, wcols(c, k)]),
                        lambda k: (ahi[:, k, a0:a0 + cols], alo[:, k, a0:a0 + cols]),
                        kc).then_inc(done.sem, 1)

            def first_tile(c, t):
                a = slice(c0 + t * step, c0 + (t + 1) * step)
                return (ps[:, 2 * c + t if nts == 2 else c, 0:step],
                        lambda k: (ring.hi[0][:, wcols(c, k)], ring.lo[0][:, wcols(c, k)]),
                        lambda k: (hhi[:, k, a], hlo[:, k, a]), s.qk_done)

            pe.wait_ge(ring.ready[0].sem, ring.ready[0].d.next(pe))
            pe.wait_ge(s.qk_out.sem, s.qk_out.f.next(pe, 2 * nts))
            products_together(pe, [first_tile(c, t) for c in range(2) for t in range(nts)], KD, chunk_wait)
            for n in range(1, n_qkv):
                pe.wait_ge(ring.ready[slot(n)].sem, ring.ready[slot(n)].d.next(pe))
                if slabs[n][0] == "qk":
                    for c in range(2):
                        for t in range(nts):
                            pe.wait_ge(s.qk_out.sem, s.qk_out.f.next(pe))
                            bank = 2 * c + t if nts == 2 else 2 * (n % 2) + c
                            channel_tile(n, c, bank, c0 + t * step, step, KD, hhi, hlo, s.qk_done)
                else:
                    for c in range(n_tok // P):
                        pe.wait_ge(s.v_out.sem, s.v_out.f.next(pe))
                        i = c + (n - n_qkv + 2) * (n_tok // P)
                        w = slot(n)
                        a = slice(c0 + c * P, c0 + (c + 1) * P)
                        product(pe, ps[:, 4 + i % 4, 0:SC],
                                lambda k: (hhi[:, k, a], hlo[:, k, a]),
                                lambda k: (ring.hi[w][:, k * SC:(k + 1) * SC], ring.lo[w][:, k * SC:(k + 1) * SC]),
                                KD).then_inc(s.v_done.sem, 1)
            if b is None:
                return
            pe.wait_ge(s.qk_out.sem, s.qk_out.drained(pe))
            pe.wait_ge(s.v_out.sem, s.v_out.drained(pe))
            for j in range(2):
                n = n_qkv + 3 * j
                pe.wait_ge(s.bg_out.sem, s.bg_out.drained(pe))
                for m, (done, out, bank, tiles, a0, cols) in enumerate((
                        (s.cg_done, s.cg_out, 0, 3, 0, HT), (s.hv_done, s.hv_out, 3, 3, 0, HT),
                        (s.bg_done, s.bg_out, 6, 2, 1, NT))):
                    pe.wait_ge(ring.ready[slot(n + m)].sem, ring.ready[slot(n + m)].d.next(pe))
                    for c in range(2):
                        for t in range(tiles):
                            pe.wait_ge(out.sem, out.f.next(pe))
                            channel_tile(n + m, c, bank + t, a0 + t * cols, cols, KD, hhi, hlo, done)
            for x in (s.cg_out, s.hv_out, s.bg_out):
                pe.wait_ge(x.sem, x.drained(pe))
            pe.wait_ge(s.u_ready.sem, s.u_ready.d.next(pe, 4))
            n = n_qkv + 6
            with repeat(pe, 4, {s.gb_out.f: 4, s.yb_out.f: 4, s.ga_out.f: 4, **ring.per((1, 1, 1), "use")}):
                pe.wait_ge(s.yb_out.sem, s.yb_out.drained(pe))
                for m, (done, out, bank, kc, a0, ahi, alo) in enumerate((
                        (s.gb_done, s.gb_out, 0, KD, 1, hhi, hlo), (s.yb_done, s.yb_out, 4, KA, 0, uhi, ulo),
                        (s.ga_done, s.ga_out, 6, KD, 1, hhi, hlo))):
                    pe.wait_ge(ring.ready[slot(n + m)].sem, ring.ready[slot(n + m)].d.next(pe))
                    for c in range(2):
                        for t in range(2):
                            pe.wait_ge(out.sem, out.f.next(pe))
                            channel_tile(n + m, c, bank + (2 * c if m == 0 else 0) + t, a0 + t * NT, NT, kc,
                                         ahi, alo, done)


def make_attention_signals(env):
    s = Env()
    s.q_in, s.k_in, s.v_in = Signal(env, "q_in"), Signal(env, "k_in"), Signal(env, "v_in")
    s.tab_in = [Signal(env, f"att_tab_in{i}") for i in range(2)]
    s.q_rounded, s.k_rounded, s.v_rounded = (Signal(env, n) for n in ("q_rounded", "k_rounded", "v_rounded"))
    s.q_split, s.k_split, s.v_split = (Signal(env, n) for n in ("q_split", "k_split", "v_split"))
    s.zeroed = Signal(env, "att_zeroed")
    s.scored = Signal(env, "scored")
    s.biased = Signal(env, "biased", 1)
    s.peaked = Signal(env, "peaked")
    s.edge_step = Signal(env, "edge_step")
    s.score_seen = Signal(env, "score_seen")
    s.exped = Signal(env, "exped")
    s.turned = Signal(env, "turned")
    s.p_rounded = Signal(env, "p_rounded")
    s.p_split = Signal(env, "p_split", 2)
    s.summed = Signal(env, "summed")
    s.weighed = Signal(env, "weighed")
    s.ot_out = Signal(env, "att_ot_out")
    s.folder_set = Signal(env, "att_folder_set")
    s.folded = Signal(env, "att_folded")
    s.o_out = Signal(env, "att_o_out", 2)
    s.att_stored = [Signal(env, f"att_stored{i}", 16) for i in range(2)]
    s.ada_in = [Signal(env, f"att_ada_in{i}") for i in range(2)]
    s.ada_summed = Signal(env, "att_ada_summed")
    s.ada_used = Signal(env, "att_ada_used", 2)
    s.ada_out, s.mod_step = Signal(env, "att_ada_out"), Signal(env, "att_mod_step")
    return s


def attention(nc, env, io):
    s = env.asig
    nk = NTOK // P
    width = WIN + CTX
    ada0 = 2 * D // SC
    ada_steps = {11: 0, 15: 1}
    ada_col = 2 * P + DH
    zero0 = TCOLS

    def span(n):
        r = 2 * n
        if r < WIN_H // 2:
            return 0, WIN_H - 1 - r, WIN_H * GRID_W
        if r > ROWS - WIN_H // 2 - 2:
            return ROWS - WIN_H, ROWS - 1 - r, WIN_H * GRID_W
        return r - WIN_H // 2, None, WIN

    with ExitStack() as ctx:
        sb = lambda n, sh, d=F32: ctx.enter_context(nc.sbuf_tensor("att_" + n, sh, d))
        qr, kr, vr = sb("qr", [P, SEQ]), sb("kr", [P, NTOK]), sb("vr", [P, nk, DH])
        qhi = [sb(f"qhi{i}", [P, SEQ], F32R) for i in range(2)]
        qlo = [sb(f"qlo{i}", [P, SEQ], F32R) for i in range(2)]
        kk = [sb(f"kk{i}", [P, NTOK], F32R) for i in range(2)]
        vv = [sb(f"vv{i}", [P, nk, 2 * DH], F32R) for i in range(2)]
        tab = [sb(f"tab{i}", [P, TCOLS + CTX]) for i in range(2)]
        sc = [sb(f"sc{i}", [P, width]) for i in range(2)]
        pt = [sb(f"pt{i}", [P, width // P, 2, P], F32R) for i in range(2)]
        peak, peak2, npeak = sb("peak", [P, 32]), sb("peak2", [P, 32]), sb("npeak", [P, 32])
        den, rden = sb("den", [P, 32]), sb("rden", [P, 32])
        ot = [sb(f"ot{i}", [P, 2 * P]) for i in range(2)]
        folder = sb("folder", [P, DH])
        out = [sb(f"out{i}", [P, PAIRS, DH]) for i in range(2)]
        aw = [sb(f"aw{i}", [P, SLAB]) for i in range(2)]
        asum = [sb(f"asum{i}", [P, SC]) for i in range(2)]
        modt = sb("modt", [P, 4 * KD])
        ps_s = ctx.enter_context(nc.psum_tensor("ps_s", [P, 1024], F32))
        ps_t = ctx.enter_context(nc.psum_tensor("ps_t", [P, 2, 1024], F32))
        ps_o = ctx.enter_context(nc.psum_tensor("ps_o", [P, 2, 512], F32))
        block = ctx.enter_context(nc.Block())

        def rest_q(eng, i):
            eng.wait_ge(s.q_rounded.sem, s.q_rounded.d.next(eng, 2))
            eng.tensor_tensor(qlo[i][:], qr[:], qhi[i][:].bitcast(F32), ALU.subtract).then_inc(s.q_split.sem, 1)

        def rest_k(eng, i):
            eng.wait_ge(s.k_rounded.sem, s.k_rounded.d.next(eng, 2))
            eng.wait_ge(s.q_split.sem, s.q_split.d.next(eng))
            eng.tensor_tensor(kk[i][64:128, :], kr[64:128, :], kk[i][64:128, :].bitcast(F32),
                              ALU.subtract).then_inc(s.k_split.sem, 1)

        def rest_v(eng, i):
            eng.wait_ge(s.v_rounded.sem, s.v_rounded.d.next(eng))
            eng.wait_ge(s.k_split.sem, s.k_split.d.next(eng))
            eng.tensor_tensor(vv[i][:, :, DH:2 * DH], vr[:], vv[i][:, :, 0:DH].bitcast(F32),
                              ALU.subtract).then_inc(s.v_split.sem, 1)

        @block.gpsimd
        def _(pool):
            for i in range(2):
                pool.memset(tab[i][:, zero0:zero0 + CTX], 0.0).then_inc(s.zeroed.sem, 1)
            for x, n in ((s.q_rounded, 2), (s.q_split, 1), (s.k_rounded, 2), (s.k_split, 1), (s.v_rounded, 1)):
                x.d.skip(pool, n)

            def load(n):
                pool.dma_start(aw[n % 2][:].rearrange("p (k c) -> p k c", k=KD),
                               slab(io["w_ada"][0], KD, (ada0 + n) * SC, SC)).then_inc(s.ada_in[n % 2].sem, 16)

            load(0)
            for n in range(2 * HEADS):
                if n % 2 == 0 and n // 2 + 1 < HEADS:
                    i = (n // 2 + 1) % 2
                    rest_q(pool, i)
                    rest_k(pool, i)
                    rest_v(pool, i)
                if n + 1 < 2 * HEADS:
                    load(n + 1)
                pool.wait_ge(s.ada_used.sem, s.ada_used.f.next(pool))
                pool.wait_ge(s.ada_in[n % 2].sem, s.ada_in[n % 2].d.next(pool, 16))
                w = aw[n % 2]
                c = env.csil[:, 0:KD].unsqueeze(2).broadcast_to([P, KD, SC])
                w3 = w[:].rearrange("p (k c) -> p k c", k=KD)
                pool.tensor_tensor(w3, w3, c, ALU.mult).then_inc(s.ada_summed.sem, 1)
                for half in (4 * SC, 2 * SC, SC):
                    pool.wait_ge(s.ada_summed.sem, s.ada_summed.d.next(pool))
                    total = w[:, 0:half] if half > SC else asum[n % 2][:]
                    pool.tensor_tensor(total, w[:, 0:half], w[:, half:2 * half], ALU.add).then_inc(s.ada_summed.sem, 1)
                pool.wait_ge(s.ada_summed.sem, s.ada_summed.d.next(pool))

        @block.sync
        def _(sp):
            for h in range(HEADS):
                if h >= 1:
                    sp.wait_ge(s.q_split.sem, s.q_split.d.next(sp))
                    sp.wait_ge(s.k_split.sem, s.k_split.d.next(sp))
                    sp.wait_ge(s.v_split.sem, s.v_split.d.next(sp))
                for half in (0, 64):
                    sp.dma_start(qr[half:half + 64, :], env.qk_d[h * DH:(h + 1) * DH, 0:SEQ]).then_inc(s.q_in.sem, 16)
                for half in (0, 64):
                    sp.dma_start(kr[half:half + 64, :],
                                 env.qk_d[ATT_W + h * DH:ATT_W + (h + 1) * DH, :]).then_inc(s.k_in.sem, 16)
                sp.dma_start(vr[:], env.v_d[:, h * DH:(h + 1) * DH].rearrange("(t p) d -> p t d", p=P)).then_inc(s.v_in.sem, 16)
                if h >= 2:
                    sp.wait_ge(s.biased.sem, s.biased.d.next(sp, PAIRS))
                sp.dma_start(tab[h % 2][:, 0:TCOLS], env.bt_d[h]).then_inc(s.tab_in[h % 2].sem, 16)
            sp.wait_ge(s.biased.sem, s.biased.d.next(sp, 2 * PAIRS))

        def round_q(act, i, half):
            if half == 0:
                act.wait_ge(s.q_in.sem, s.q_in.d.next(act, 32))
            a = slice(half * (SEQ // 2), (half + 1) * (SEQ // 2))
            act.activation(qhi[i][:, a], qr[:, a], ACT.Copy).then_inc(s.q_rounded.sem, 1)

        def round_k(act, i, half):
            if half == 0:
                act.wait_ge(s.k_in.sem, s.k_in.d.next(act, 32))
            a = slice(half * (NTOK // 2), (half + 1) * (NTOK // 2))
            act.activation(kk[i][:, a], kr[:, a], ACT.Copy).then_inc(s.k_rounded.sem, 1)

        def round_v(act, i):
            act.wait_ge(s.v_in.sem, s.v_in.d.next(act, 16))
            act.activation(vv[i][:, :, 0:DH], vr[:], ACT.Copy).then_inc(s.v_rounded.sem, 1)

        @block.scalar
        def _(act):
            def expo(g):
                w = span(g % PAIRS)[2] + CTX
                act.wait_ge(s.peaked.sem, s.peaked.d.next(act))
                act.activation(sc[g % 2][:, 0:w], sc[g % 2][:, 0:w], ACT.Exp, bias=npeak[:, g:g + 1],
                               accum_out=den[:, g:g + 1]).then_inc(s.exped.sem, 1)

            def round_p(g):
                w = span(g % PAIRS)[2] + CTX
                act.wait_ge(s.turned.sem, s.turned.d.next(act))
                act.activation(pt[g % 2][:, 0:w // P, 0, :], ps_t[:, g % 2, 0:w].rearrange("p (c q) -> p c q", q=P),
                               ACT.Copy).then_inc(s.p_rounded.sem, 1)

            def unload(g):
                act.wait_ge(s.weighed.sem, s.weighed.d.next(act))
                act.activation(ot[g % 2][:], ps_o[:, g % 2, 0:2 * P], ACT.Copy).then_inc(s.ot_out.sem, 1)

            def store(h, i):
                act.wait_ge(s.o_out.sem, s.o_out.d.next(act, PAIRS))
                act.dma_start(bass.AP(tensor=env.att_d.tensor, offset=(h + i) * DH,
                                      ap=[[ATT_W, P], [P * ATT_W, PAIRS], [1, DH]]),
                              out[i][:]).then_inc(s.att_stored[i].sem, 16)

            def two_heads(h, last):
                expo(0)
                for g in range(2 * PAIRS):
                    nxt = (g // PAIRS + 1) % 2
                    if not (last and g >= PAIRS):
                        if g % PAIRS in (2, 3):
                            round_q(act, nxt, g % PAIRS - 2)
                        if g % PAIRS in (4, 5):
                            round_k(act, nxt, g % PAIRS - 4)
                        if g % PAIRS == 6:
                            round_v(act, nxt)
                    round_p(g)
                    if g + 1 < 2 * PAIRS:
                        expo(g + 1)
                    if g >= 1:
                        unload(g - 1)
                    if g == PAIRS + 2:
                        store(h, 0)
                unload(2 * PAIRS - 1)
                store(h, 1)

            for half in range(2):
                round_q(act, 0, half)
            for half in range(2):
                round_k(act, 0, half)
            round_v(act, 0)
            with repeat(act, HEADS // 2 - 1, {
                    s.q_in.d: 64, s.k_in.d: 64, s.v_in.d: 32, s.peaked.d: 32, s.turned.d: 32,
                    s.weighed.d: 32,
                    s.o_out.d: 32}) as i:
                two_heads(i * 2, False)
            two_heads(HEADS - 2, True)
            for i in range(2):
                act.wait_ge(s.att_stored[i].sem, s.att_stored[i].d.next(act, 16 * HEADS // 2))

        @block.vector
        def _(dve):
            def bias(g):
                n = g % PAIRS
                _, j, w = span(n)
                t = tab[g // PAIRS]
                dve.wait_ge(s.scored.sem, s.scored.d.next(dve))
                dve.sem_inc(s.score_seen.sem, 1)
                if j is None:
                    dve.tensor_tensor_reduce(sc[g % 2][:, 0:w + CTX], ps_s[:, 0:w + CTX],
                                             t[:, TROWS * GRID_W:TCOLS + CTX], 1.0, NEG, ALU.add, ALU.max,
                                             peak[:, g:g + 1]).then_inc(s.biased.sem, 1)
                    dve.wait_ge(s.biased.sem, s.biased.d.next(dve))
                    dve.tensor_scalar(npeak[:, g:g + 1], peak[:, g:g + 1], -1.0, None, ALU.mult).then_inc(s.peaked.sem, 1)
                    return
                dve.tensor_tensor_reduce(sc[g % 2][:, 0:w], ps_s[:, 0:w],
                                         t[:, j * GRID_W:j * GRID_W + w], 1.0, NEG, ALU.add, ALU.max,
                                         peak[:, g:g + 1]).then_inc(s.edge_step.sem, 1)
                dve.tensor_tensor_reduce(sc[g % 2][:, w:w + CTX], ps_s[:, w:w + CTX],
                                         t[:, zero0:zero0 + CTX], 1.0, NEG, ALU.add, ALU.max,
                                         peak2[:, g:g + 1]).then_inc(s.biased.sem, 1)
                dve.wait_ge(s.edge_step.sem, s.edge_step.d.next(dve))
                dve.wait_ge(s.biased.sem, s.biased.d.next(dve))
                dve.tensor_scalar(npeak[:, g:g + 1], peak[:, g:g + 1], peak2[:, g:g + 1], -1.0, ALU.max,
                                  ALU.mult).then_inc(s.peaked.sem, 1)

            def rest_p(g):
                w = span(g % PAIRS)[2] + CTX
                dve.wait_ge(s.p_rounded.sem, s.p_rounded.d.next(dve))
                x = pt[g % 2][:, 0:w // P]
                dve.tensor_tensor(x[:, :, 1, :], ps_t[:, g % 2, 0:w].rearrange("p (c q) -> p c q", q=P),
                                  x[:, :, 0, :].bitcast(F32), ALU.subtract).then_inc(s.p_split.sem, 1)

            def inverse(g):
                dve.wait_ge(s.exped.sem, s.exped.d.next(dve))
                dve.reciprocal(rden[:, g:g + 1], den[:, g:g + 1]).then_inc(s.summed.sem, 1)

            def finish(g, pair=None):
                i, n = g // PAIRS, g % PAIRS
                if n == 0:
                    dve.wait_ge(s.att_stored[i].sem, s.att_stored[i].f.next(dve, 16))
                dve.wait_ge(s.folded.sem, s.folded.d.next(dve))
                if g == 2 * PAIRS - 1:
                    dve.tensor_copy(modt[:, 24:32] if pair is None else modt[:, bass.ds(pair * 8, 8)],
                                    ps_o[:, 1, ada_col:ada_col + 8]).then_inc(s.ada_out.sem, 1)
                dve.wait_ge(s.summed.sem, s.summed.d.next(dve))
                dve.tensor_scalar(out[i][:, n, :], ps_o[:, g % 2, 2 * P:2 * P + DH], rden[:, g:g + 1], None,
                                  ALU.mult).then_inc(s.o_out.sem, 1)

            def two_heads(i):
                last = i is None
                dve.wait_ge(s.tab_in[0].sem, s.tab_in[0].d.next(dve, 16))
                bias(0)
                for g in range(2 * PAIRS):
                    if g + 1 < 2 * PAIRS:
                        if g + 1 == PAIRS:
                            dve.wait_ge(s.tab_in[1].sem, s.tab_in[1].d.next(dve, 16))
                        bias(g + 1)
                    rest_p(g)
                    inverse(g)
                    if g >= 2:
                        finish(g - 2)
                finish(2 * PAIRS - 2)
                finish(2 * PAIRS - 1, i)

            dve.wait_ge(s.zeroed.sem, s.zeroed.d.next(dve, 2))
            dve.tensor_tensor(folder[:], env.ident[:, 0:DH], env.ident[:, DH:2 * DH], ALU.add).then_inc(s.folder_set.sem, 1)
            rest_q(dve, 0)
            rest_k(dve, 0)
            rest_v(dve, 0)
            with repeat(dve, HEADS // 2 - 1, {
                    s.tab_in[0].d: 16, s.tab_in[1].d: 16,
                    s.scored.d: 32, s.biased.d: 32, s.edge_step.d: 8, s.p_rounded.d: 32, s.exped.d: 32,
                    s.folded.d: 32, s.summed.d: 32,
                    s.att_stored[0].f: 16, s.att_stored[1].f: 16}) as i:
                two_heads(i)
            two_heads(None)
            dve.wait_ge(s.ada_out.sem, s.ada_out.d.next(dve, HEADS // 2))
            dve.tensor_tensor(modt[:], modt[:], env.param[:, 16:48], ALU.add).then_inc(s.mod_step.sem, 1)
            dve.wait_ge(s.mod_step.sem, s.mod_step.d.next(dve))
            dve.tensor_tensor(env.gate1[:], modt[:, 0:8], env.param[:, 56:64], ALU.mult)
            dve.tensor_copy(env.shift2[:], modt[:, 8:16])
            dve.scalar_tensor_tensor(out=env.scale2[:], in0=modt[:, 16:24], scalar=1.0, in1=env.param[:, 64:72],
                                     op0=ALU.add, op1=ALU.mult)
            dve.tensor_tensor(env.gate2[:], modt[:, 24:32], env.param[:, 72:80], ALU.mult).then_inc(s.mod_step.sem, 1)

        @block.tensor
        def _(pe):
            def score(g):
                i, n = g // PAIRS, g % PAIRS
                row, _, w = span(n)
                if n == 0:
                    pe.wait_ge(s.q_split.sem, s.q_split.d.next(pe))
                    pe.wait_ge(s.k_split.sem, s.k_split.d.next(pe))
                    pe.wait_ge(s.v_split.sem, s.v_split.d.next(pe))
                pe.wait_ge(s.biased.sem, s.biased.f.next(pe))
                k0 = row * GRID_W
                for a, b, c in ((0, 512, k0), (512, w, k0 + 512), (w, w + CTX, SEQ)):
                    if a < b:
                        for q, first in ((qhi, True), (qlo, False)):
                            last = pe.matmul(ps_s[:, a:b], q[i][:, n * P:(n + 1) * P],
                                             kk[i][:, c:c + b - a], start=first, stop=not first)
                last.then_inc(s.scored.sem, 1)

            def turn(g):
                w = span(g % PAIRS)[2] + CTX
                pe.wait_ge(s.exped.sem, s.exped.d.next(pe))
                pe.wait_ge(s.p_split.sem, s.p_split.f.next(pe))
                for c in range(w // P):
                    last = pe.transpose(ps_t[:, g % 2, c * P:(c + 1) * P], sc[g % 2][:, c * P:(c + 1) * P], env.ident[:])
                last.then_inc(s.turned.sem, 1)

            def ada(g):
                a = ada_steps[g % PAIRS]
                pe.wait_ge(s.ada_summed.sem, s.ada_summed.d.next(pe, 4))
                m = ada_col + (g // PAIRS) * 4 + a * 2
                for c in range(2):
                    last = pe.matmul(ps_o[:, 1, m + c:m + c + 1], asum[a][:, c * P:(c + 1) * P],
                                     env.ones[:, 0:1], start=True, stop=True)
                last.then_inc(s.ada_used.sem, 1)

            def weigh(g):
                i, n = g // PAIRS, g % PAIRS
                row, _, w = span(n)
                tiles = [row * GRID_W // P + c for c in range(w // P)] + [SEQ // P + c for c in range(CTX // P)]
                pe.wait_ge(s.p_split.sem, s.p_split.d.next(pe))
                pe.wait_ge(s.o_out.sem, s.o_out.f.next(pe))
                if g % PAIRS in ada_steps:
                    ada(g)
                for c, t in enumerate(tiles):
                    last = pe.matmul(ps_o[:, g % 2, 0:2 * P], vv[i][:, t, :],
                                     pt[g % 2][:, c, :, :].rearrange("p a q -> p (a q)"), start=(c == 0),
                                     stop=(c == len(tiles) - 1))
                last.then_inc(s.weighed.sem, 1)

            def fold(g):
                pe.wait_ge(s.ot_out.sem, s.ot_out.d.next(pe))
                pe.matmul(ps_o[:, g % 2, 2 * P:2 * P + DH], ot[g % 2][:, 0:P], folder[:], start=True, stop=False)
                pe.matmul(ps_o[:, g % 2, 2 * P:2 * P + DH], ot[g % 2][:, P:2 * P], folder[:], start=False,
                          stop=True).then_inc(s.folded.sem, 1)

            pe.wait_ge(s.folder_set.sem, s.folder_set.d.next(pe))

            with repeat(pe, HEADS // 2, {
                    s.q_split.d: 2, s.k_split.d: 2, s.v_split.d: 2, s.biased.f: 32, s.exped.d: 32,
                    s.p_split.f: 32, s.p_split.d: 32, s.o_out.f: 32,
                    s.ada_summed.d: 4 * 4, s.ot_out.d: 32}):
                score(0)
                for g in range(2 * PAIRS):
                    if g + 1 < 2 * PAIRS:
                        score(g + 1)
                    turn(g)
                    if g >= 1:
                        weigh(g - 1)
                    if g >= 2:
                        fold(g - 2)
                weigh(2 * PAIRS - 1)
                fold(2 * PAIRS - 2)
                fold(2 * PAIRS - 1)


class Norm:

    def __init__(self, env, name):
        self.squared = Signal(env, f"{name}_squared")
        self.added = Signal(env, f"{name}_added", 2)
        self.summed = Signal(env, f"{name}_summed")
        self.rooted = Signal(env, f"{name}_rooted")
        self.inverted = Signal(env, f"{name}_inverted")
        self.spread_out = Signal(env, f"{name}_spread_out")

    def add(self, pool, k, acc, sq):
        pool.wait_ge(self.squared.sem, self.squared.d.next(pool))
        if k == 0:
            pool.sem_inc(self.added.sem, 1)
            self.added.d.skip(pool, 1)
            return
        if k >= 2:
            pool.wait_ge(self.added.sem, self.added.d.next(pool))
        pool.tensor_tensor(acc[:], acc[:], sq[:], ALU.add).then_inc(self.added.sem, 1)
        if k == KD - 1:
            pool.wait_ge(self.added.sem, self.added.d.next(pool))

    def sums(self, pe, env, ps, bank, acc):
        pe.wait_ge(self.added.sem, self.added.d.next(pe, KD))
        for t in range(BLK // P):
            last = pe.matmul(ps[:, bank, t:t + 1], acc[:, t * P:(t + 1) * P], env.ones[:, 0:1], start=True, stop=True)
        last.then_inc(self.summed.sem, 1)

    def root(self, act, env, ps, bank, rc):
        act.wait_ge(self.summed.sem, self.summed.d.next(act))
        act.activation(rc[:], ps[:, bank, 0:BLK // P], ACT.Sqrt, scale=1.0 / D,
                       bias=env.eps[:, 0:1]).then_inc(self.rooted.sem, 1)

    def inverse(self, dve, rc):
        dve.wait_ge(self.rooted.sem, self.rooted.d.next(dve))
        dve.reciprocal(rc[:], rc[:]).then_inc(self.inverted.sem, 1)

    def spread(self, pe, env, ps, banks, rc):
        pe.wait_ge(self.inverted.sem, self.inverted.d.next(pe))
        for t in range(BLK // P):
            last = pe.matmul(ps[:, banks[t // 4], (t % 4) * P:(t % 4 + 1) * P], rc[:, t:t + 1].broadcast_to([P, P]),
                             env.ident[:], start=True, stop=True)
        last.then_inc(self.spread_out.sem, 1)


def make_merge_signals(env):
    s = Env()
    s.att_in = [Signal(env, f"m_att_in{i}") for i in range(4)]
    s.att_turned, s.att_rounded = Signal(env, "m_att_turned"), Signal(env, "m_att_rounded")
    s.att_split = Signal(env, "m_att_split", 2)
    s.gate_in = [Signal(env, f"m_gate_in{i}") for i in range(2)]
    s.ya_done, s.ya_out = Signal(env, "ya_done"), Signal(env, "ya_out", 4)
    s.z_summed, s.z_rounded = Signal(env, "z_summed"), Signal(env, "z_rounded")
    s.z_split = Signal(env, "z_split", 2)
    s.y_done, s.y_out = Signal(env, "y_done"), Signal(env, "y_out", 4)
    s.post, s.next = Norm(env, "m_post"), Norm(env, "m_next")
    s.x_in = [Signal(env, f"m_x_in{i}") for i in range(2)]
    s.y_scaled = Signal(env, "m_y_scaled")
    s.x_sum = Signal(env, "m_x_sum")
    s.r_turned, s.r_out = Signal(env, "m_r_turned"), Signal(env, "m_r_out")
    s.stored, s.r_stored = Signal(env, "m_stored"), Signal(env, "m_r_stored")
    return s


def merge(nc, env, io, b):
    ring, s = env.ring, env.msig
    t0 = b * BLK
    tag = f"m{b}"
    WC = 4 * P
    slabs = [slab(io["w_branch_attn"][0], KA, j * WC, WC) for j in range(2)]
    slabs += [slab(io["w_out"][0], KD, j * SC, SC) for j in range(4)]
    with ExitStack() as ctx:
        sb = lambda n, sh, d=F32: ctx.enter_context(nc.sbuf_tensor(f"{n}_{tag}", sh, d))
        ring.tensors(nc, ctx, tag)
        zhi, zlo = sb("z_hi", [P, KD, BLK], F32R), sb("z_lo", [P, KD, BLK], F32R)
        atok = [sb(f"atok{i}", [P, ATT_W]) for i in range(4)]
        ga = [sb(f"ga{i}", [P, BLK]) for i in range(2)]
        cb = [sb(f"cb{i}", [P, BLK]) for i in range(2)]
        acc = sb("acc", [P, BLK])
        rc = sb("rc", [P, BLK // P])
        rrow = sb("rrow", [BLK // P, P])
        with ExitStack() as inner:
            ahi = inner.enter_context(nc.sbuf_tensor(f"a_hi_{tag}", [P, KA, BLK], F32R))
            alo = inner.enter_context(nc.sbuf_tensor(f"a_lo_{tag}", [P, KA, BLK], F32R))
        y = sb("y", [P, KD, BLK])
        ps = ctx.enter_context(nc.psum_tensor(f"ps_{tag}", [P, 8, 512], F32))
        y_banks = (0, 1, 6, 7)
        slot = lambda n: n % RING
        block = ctx.enter_context(nc.Block())

        @block.sync
        def _(sp):
            for t in range(BLK // P):
                if t >= 4:
                    sp.wait_ge(s.att_turned.sem, s.att_turned.d.next(sp))
                sp.dma_start(atok[t % 4][:], env.att_d[t0 + t * P:t0 + (t + 1) * P, :]).then_inc(s.att_in[t % 4].sem, 16)
                if t == 3:
                    ring.load(sp, slot(0), slabs[0])
            for n in range(1, RING):
                ring.load(sp, slot(n), slabs[n])
            for k in range(KD):
                if k == 4:
                    ring.load(sp, slot(RING), slabs[RING])
                sp.wait_ge(s.z_split.sem, s.z_split.f.next(sp))
                sp.dma_start(ga[k % 2][:], env.ga_d[k * P:(k + 1) * P, t0:t0 + BLK]).then_inc(s.gate_in[k % 2].sem, 16)
                sp.dma_start(cb[k % 2][:], env.cb_d[k * P:(k + 1) * P, t0:t0 + BLK]).then_inc(s.gate_in[k % 2].sem, 16)
            s.att_turned.d.skip(sp, 4)
            for n in range(RING + 1, len(slabs)):
                ring.load(sp, slot(n), slabs[n])
            sp.wait_ge(s.z_split.sem, s.z_split.drained(sp))
            for k in range(KD):
                if k >= 2:
                    sp.wait_ge(s.x_sum.sem, s.x_sum.d.next(sp))
                sp.dma_start(cb[k % 2][:], env.xt_d[k * P:(k + 1) * P, t0:t0 + BLK]).then_inc(s.x_in[k % 2].sem, 16)
            sp.wait_ge(s.x_sum.sem, s.x_sum.d.next(sp, 2))

        @block.gpsimd
        def _(pool):
            for k in range(KD):
                s.post.add(pool, k, acc, ga[k % 2])
            pool.wait_ge(s.post.summed.sem, s.post.summed.d.next(pool))
            for k in range(KD):
                s.next.add(pool, k, acc, ga[k % 2])

        @block.scalar
        def _(act):
            for t in range(BLK // P):
                act.wait_ge(s.att_turned.sem, s.att_turned.d.next(act))
                act.activation(ahi[:, :, t * P:(t + 1) * P], ps[:, t % 2, :].rearrange("p (k t) -> p k t", k=KA),
                               ACT.Copy).then_inc(s.att_rounded.sem, 1)
                if t == 3:
                    ring.round(act, slot(0))
            for n in range(1, RING):
                ring.round(act, slot(n))
            for k in range(KD):
                act.wait_ge(s.z_summed.sem, s.z_summed.d.next(act))
                act.activation(zhi[:, k, :], ga[k % 2][:], ACT.Copy).then_inc(s.z_rounded.sem, 1)
                if k % 4 == 3:
                    ring.round(act, slot(k // 4), SLAB)
            act.wait_ge(s.z_split.sem, s.z_split.d.next(act, KD))
            for k in range(KD):
                act.wait_ge(s.post.added.sem, s.post.added.f.next(act))
                for t in range(2):
                    act.wait_ge(s.y_done.sem, s.y_done.d.next(act))
                    bank = y_banks[(2 * k + t) % 4]
                    act.activation(y[:, k, t * NT:(t + 1) * NT], ps[:, bank, :], ACT.Copy)
                    sq = ga[k % 2] if k else acc
                    last = act.activation(sq[:, t * NT:(t + 1) * NT], ps[:, bank, :], ACT.Square)
                    last.then_inc(s.y_out.sem, 1)
                act.wait_ge(s.y_out.sem, s.y_out.d.next(act, 2))
                act.sem_inc(s.post.squared.sem, 1)
                if k == 1:
                    ring.round(act, slot(5), SLAB)
            s.post.root(act, env, ps, 4, rc)
            for k in range(KD):
                act.wait_ge(s.next.added.sem, s.next.added.f.next(act))
                if k < 2:
                    act.wait_ge(s.post.added.sem, s.post.added.d.next(act, KD // 2))
                act.wait_ge(s.x_sum.sem, s.x_sum.d.next(act))
                act.dma_start(env.x1_d[k * P:(k + 1) * P, t0:t0 + BLK], y[:, k, :]).then_inc(s.stored.sem, 16)
                act.activation((ga[k % 2] if k else acc)[:], y[:, k, :], ACT.Square).then_inc(s.next.squared.sem, 1)
            s.next.root(act, env, ps, 5, rc)
            act.wait_ge(s.r_out.sem, s.r_out.d.next(act))
            act.dma_start(env.r2_d[t0:t0 + BLK].rearrange("(t p) -> t p", p=P), rrow[:]).then_inc(s.r_stored.sem, 16)
            act.wait_ge(s.stored.sem, s.stored.d.next(act, 16 * KD))
            act.wait_ge(s.r_stored.sem, s.r_stored.d.next(act, 16))

        @block.vector
        def _(dve):
            for t in range(BLK // P):
                dve.wait_ge(s.att_rounded.sem, s.att_rounded.d.next(dve))
                dve.tensor_tensor(alo[:, :, t * P:(t + 1) * P], ps[:, t % 2, :].rearrange("p (k t) -> p k t", k=KA),
                                  ahi[:, :, t * P:(t + 1) * P].bitcast(F32), ALU.subtract).then_inc(s.att_split.sem, 1)
                if t == 3:
                    ring.rest(dve, slot(0))
            for n in range(1, RING):
                ring.rest(dve, slot(n))

            def rest_z(k):
                dve.wait_ge(s.z_rounded.sem, s.z_rounded.d.next(dve))
                dve.tensor_tensor(zlo[:, k, :], ga[k % 2][:], zhi[:, k, :].bitcast(F32),
                                  ALU.subtract).then_inc(s.z_split.sem, 1)

            for k in range(KD):
                dve.wait_ge(s.gate_in[k % 2].sem, s.gate_in[k % 2].d.next(dve, 32))
                for t in range(2):
                    dve.wait_ge(s.ya_done.sem, s.ya_done.d.next(dve))
                    dve.tensor_tensor(ga[k % 2][:, t * NT:(t + 1) * NT], ps[:, 2 + (2 * k + t) % 4, :],
                                      ga[k % 2][:, t * NT:(t + 1) * NT], ALU.mult).then_inc(s.ya_out.sem, 1)
                dve.wait_ge(s.ya_out.sem, s.ya_out.d.next(dve, 2))
                dve.tensor_tensor(ga[k % 2][:], ga[k % 2][:], cb[k % 2][:], ALU.add).then_inc(s.z_summed.sem, 1)
                rest_z(k)
                if k % 4 == 3:
                    ring.rest(dve, slot(k // 4))
            ring.rest(dve, slot(5))
            s.post.inverse(dve, rc)
            dve.wait_ge(s.post.spread_out.sem, s.post.spread_out.d.next(dve))
            r = ps[:, 2:4, :].rearrange("p a b -> p (a b)")
            for k in range(KD):
                dve.wait_ge(s.x_in[k % 2].sem, s.x_in[k % 2].d.next(dve, 16))
                if k == 0:
                    dve.wait_ge(s.y_out.sem, s.y_out.d.next(dve, 2 * KD))
                dve.scalar_tensor_tensor(out=y[:, k, :], in0=y[:, k, :], scalar=env.gate1[:, k:k + 1], in1=r,
                                         op0=ALU.mult, op1=ALU.mult).then_inc(s.y_scaled.sem, 1)
                dve.wait_ge(s.y_scaled.sem, s.y_scaled.d.next(dve))
                dve.tensor_tensor(y[:, k, :], y[:, k, :], cb[k % 2][:], ALU.add).then_inc(s.x_sum.sem, 1)
            s.next.inverse(dve, rc)
            dve.wait_ge(s.r_turned.sem, s.r_turned.d.next(dve))
            dve.tensor_copy(rrow[:], ps[0:BLK // P, 6, 0:P]).then_inc(s.r_out.sem, 1)

        @block.tensor
        def _(pe):
            for t in range(BLK // P):
                pe.wait_ge(s.att_in[t % 4].sem, s.att_in[t % 4].d.next(pe, 16))
                pe.wait_ge(s.att_split.sem, s.att_split.f.next(pe))
                for k in range(KA):
                    last = pe.transpose(ps[:, t % 2, k * P:(k + 1) * P], atok[t % 4][:, k * P:(k + 1) * P], env.ident[:])
                last.then_inc(s.att_turned.sem, 1)
            pe.wait_ge(s.att_split.sem, s.att_split.drained(pe))
            for n in range(2):
                pe.wait_ge(ring.ready[slot(n)].sem, ring.ready[slot(n)].d.next(pe))
                w = slot(n)
                for c in range(WC // P):
                    for t in range(2):
                        i = (n * (WC // P) + c) * 2 + t
                        pe.wait_ge(s.ya_out.sem, s.ya_out.f.next(pe))
                        product(pe, ps[:, 2 + i % 4, :],
                                lambda k: (ring.hi[w][:, k * WC + c * P:k * WC + (c + 1) * P],
                                           ring.lo[w][:, k * WC + c * P:k * WC + (c + 1) * P]),
                                lambda k: (ahi[:, k, t * NT:(t + 1) * NT], alo[:, k, t * NT:(t + 1) * NT]),
                                KA).then_inc(s.ya_done.sem, 1)

            def first_tile(c, t):
                w = slot(2)
                return (ps[:, y_banks[2 * c + t], :],
                        lambda k: (ring.hi[w][:, k * SC + c * P:k * SC + (c + 1) * P],
                                   ring.lo[w][:, k * SC + c * P:k * SC + (c + 1) * P]),
                        lambda k: (zhi[:, k, t * NT:(t + 1) * NT], zlo[:, k, t * NT:(t + 1) * NT]), s.y_done)

            pe.wait_ge(ring.ready[slot(2)].sem, ring.ready[slot(2)].d.next(pe))
            pe.wait_ge(s.y_out.sem, s.y_out.f.next(pe, 4))
            products_together(pe, [first_tile(c, t) for c in range(2) for t in range(2)], KD,
                              lambda k: pe.wait_ge(s.z_split.sem, s.z_split.d.next(pe)))
            for n in range(3, 6):
                pe.wait_ge(ring.ready[slot(n)].sem, ring.ready[slot(n)].d.next(pe))
                w = slot(n)
                for c in range(2):
                    for t in range(2):
                        i = ((n - 2) * 2 + c) * 2 + t
                        pe.wait_ge(s.y_out.sem, s.y_out.f.next(pe))
                        product(pe, ps[:, y_banks[i % 4], :],
                                lambda k: (ring.hi[w][:, k * SC + c * P:k * SC + (c + 1) * P],
                                           ring.lo[w][:, k * SC + c * P:k * SC + (c + 1) * P]),
                                lambda k: (zhi[:, k, t * NT:(t + 1) * NT], zlo[:, k, t * NT:(t + 1) * NT]),
                                KD).then_inc(s.y_done.sem, 1)
            pe.wait_ge(s.ya_out.sem, s.ya_out.drained(pe))
            s.post.sums(pe, env, ps, 4, acc)
            s.post.spread(pe, env, ps, (2, 3), rc)
            s.next.sums(pe, env, ps, 5, acc)
            pe.wait_ge(s.next.inverted.sem, s.next.inverted.d.next(pe))
            pe.wait_ge(s.y_out.sem, s.y_out.drained(pe))
            pe.transpose(ps[0:BLK // P, 6, 0:P], rc[:], env.ident[:]).then_inc(s.r_turned.sem, 1)


def make_ffn_signals(env):
    s = Env()
    s.cleared = Signal(env, "f_cleared")
    s.taps = Signal(env, "f_taps")
    s.g_done, s.g_out = Signal(env, "f_g_done"), Signal(env, "f_g_out", 3)
    s.conv_step = Signal(env, "f_conv_step")
    s.conv_done = Signal(env, "f_conv_done")
    s.gelu_done = Signal(env, "f_gelu_done")
    s.a_done, s.a_out = Signal(env, "f_a_done"), Signal(env, "f_a_out", 2)
    s.m_rounded, s.m_ready = Signal(env, "f_m_rounded"), Signal(env, "f_m_ready")
    s.d_done, s.d_out = Signal(env, "f_d_done"), Signal(env, "f_d_out", 3)
    s.post = Norm(env, "f_post")
    s.x_in = [Signal(env, f"f_x_in{i}") for i in range(2)]
    s.y_scaled, s.x_sum = Signal(env, "f_y_scaled"), Signal(env, "f_x_sum")
    s.r_out = Signal(env, "f_r_out")
    s.o_turned = Signal(env, "f_o_turned")
    s.o_out = [Signal(env, f"f_o_out{i}") for i in range(2)]
    s.o_stored = [Signal(env, f"f_o_stored{i}") for i in range(3)]
    return s


def ffn(nc, env, io, out, b):
    ring, hl, s = env.ring, env.hload, env.fsig
    t0 = b * BLK
    tag = f"f{b}"
    w_up, w_down = io["w_up"][0], io["w_down"][0]
    G, DN, A = 0, 1, 2
    with ExitStack() as ctx:
        sb = lambda n, sh, d=F32: ctx.enter_context(nc.sbuf_tensor(f"{n}_{tag}", sh, d))
        ring.tensors(nc, ctx, tag)
        hhi, hlo = sb("h_hi", [P, KD, HW], F32R), sb("h_lo", [P, KD, HW], F32R)
        y = sb("y", [P, KD, BLK])
        mhi, mlo = sb("m_hi", [P, 2, BLK], F32R), sb("m_lo", [P, 2, BLK], F32R)
        gx = sb("gx", [P, HW])
        cv = [sb(f"cv{i}", [P, BLK]) for i in range(2)]
        taps = sb("taps", [P, 4, 2])
        rc = sb("rc", [P, BLK // P])
        ps = ctx.enter_context(nc.psum_tensor(f"ps_{tag}", [P, 8, 512], F32))
        yf = y[:].rearrange("p k t -> p (k t)")
        raw = [yf[:, (i + 1) * HW:(i + 2) * HW] for i in range(4)]
        rbuf = yf[:, 0:HW]
        params = env.param[:, 108:196].rearrange("p (r c) -> p r c", c=FC)
        block = ctx.enter_context(nc.Block())

        def up(col):
            return bass.AP(tensor=w_up.tensor, offset=w_up.offset + col, ap=[[2 * D_FF, P], [P * 2 * D_FF, KD], [1, SC]])

        def down(word):
            return bass.AP(tensor=w_down.tensor, offset=w_down.offset + word, ap=[[D, P], [P * D, 2], [1, D]])

        def ostage(i):
            g = i // 2
            return ring.stage[g // 2 % 3][:, g % 2 * D + i % 2 * NT:g % 2 * D + (i % 2 + 1) * NT]

        def store(act, g):
            half, t = g // 4, 2 * (g % 4)
            act.dma_start(out[0, t0 + t * P:t0 + (t + 2) * P, half * NT:(half + 1) * NT].rearrange("(a p) c -> p a c", p=P),
                          ring.stage[g // 2 % 3][:, g % 2 * D:(g % 2 + 1) * D].rearrange("p (a c) -> p a c", a=2)
                          ).then_inc(s.o_stored[g // 2 % 3].sem, 16)

        @block.sync
        def _(sp):
            hl.load(sp, b, env.x1_d, env.r2_d, rbuf, raw, lambda: ring.load(sp, G, up(D_FF)))
            ring.load(sp, A, up(0))
            ring.load(sp, DN, down(0))
            ring.load(sp, G, up(D_FF + SC))
            ring.load(sp, A, up(SC))
            with repeat(sp, FG - 2, ring.per((1, 1, 1), "load")) as i:
                row, g_col, a_col = (sp.snap(x) for x in ((i + 1) * (SC * D), (i + 2) * SC + D_FF, (i + 2) * SC))
                ring.load(sp, DN, down(row))
                ring.load(sp, G, up(g_col))
                ring.load(sp, A, up(a_col))
            ring.load(sp, DN, down((FG - 1) * SC * D))
            for k in range(KD):
                if k == 0:
                    sp.wait_ge(s.post.added.sem, s.post.added.d.next(sp, KD))
                if k >= 2:
                    sp.wait_ge(s.x_sum.sem, s.x_sum.d.next(sp))
                sp.dma_start(cv[k % 2][:], env.x1_d[k * P:(k + 1) * P, t0:t0 + BLK]).then_inc(s.x_in[k % 2].sem, 16)
            sp.wait_ge(s.x_sum.sem, s.x_sum.d.next(sp, 2))

        @block.gpsimd
        def _(pool):
            hl.edges(pool, b, hhi, hlo)
            pool.wait_ge(hl.ready.sem, hl.ready.d.next(pool, KD))
            pool.memset(y[:], 0.0).then_inc(s.cleared.sem, 1)
            pool.wait_ge(s.m_ready.sem, s.m_ready.d.next(pool, 2 * FG))
            for k in range(KD):
                s.post.add(pool, k, gx[:, 0:BLK], cv[k % 2])

        @block.scalar
        def _(act):
            hl.scalar(act, b, env.scale2, env.shift2, raw, hhi, lambda: ring.round(act, G))
            for x in (A, DN):
                ring.round(act, x)

            def g_part(i, more, first=False):
                act.activation(taps[:], params[:, :, bass.ds(i * 2, 2)], ACT.Copy).then_inc(s.taps.sem, 1)
                act.wait_ge(s.taps.sem, s.taps.d.next(act))
                for c in range(2):
                    if c == 1:
                        act.wait_ge(s.conv_done.sem, s.conv_done.d.next(act))
                    for t in range(3):
                        act.wait_ge(s.g_done.sem, s.g_done.d.next(act))
                        bank = 5 + t if first and c == 1 else t
                        cols = min(HT, BLK - t * HT)
                        act.activation(cv[c][:, t * HT:t * HT + cols], ps[:, bank, 0:cols], ACT.Copy,
                                       scale=taps[:, 0, c:c + 1]).then_inc(s.conv_step.sem, 1)
                        act.activation(gx[:, t * HT:(t + 1) * HT], ps[:, bank, 0:HT], ACT.Copy).then_inc(s.g_out.sem, 1)
                    if c == 1:
                        if more:
                            ring.round(act, G)
                        gelu(0)
                act.wait_ge(s.conv_done.sem, s.conv_done.d.next(act))
                gelu(1)

            def gelu(c):
                act.activation(cv[c][:], cv[c][:], ACT.Gelu_apprx_tanh, bias=taps[:, 3, c:c + 1]).then_inc(s.gelu_done.sem, 1)

            def d_part(more):
                act.wait_ge(s.d_done.sem, s.d_done.d.next(act, 16))
                if more:
                    ring.round(act, DN)

            def a_part(more):
                for c in range(2):
                    act.wait_ge(s.a_out.sem, s.a_out.d.next(act, 2))
                    act.activation(mhi[:, c, :], cv[c][:], ACT.Copy).then_inc(s.m_rounded.sem, 1)
                if more:
                    ring.round(act, A)
                act.wait_ge(s.m_ready.sem, s.m_ready.d.next(act, 2))

            g_part(0, True, True)
            a_part(True)
            with repeat(act, FG - 2, {
                    s.taps.d: 1, s.conv_done.d: 2, s.g_done.d: 6, s.d_done.d: 16, s.a_out.d: 4, s.m_ready.d: 2,
                    **ring.per((1, 1, 1), "round")}) as i:
                g_part(i + 1, True)
                d_part(True)
                a_part(True)
            g_part(FG - 1, False)
            d_part(True)
            a_part(False)
            s.d_done.d.skip(act, 16)
            s.d_out.d.skip(act, 16 * (FG - 1))
            for k in range(KD):
                act.wait_ge(s.post.added.sem, s.post.added.f.next(act))
                act.wait_ge(s.d_out.sem, s.d_out.d.next(act, 2))
                act.activation(cv[k % 2][:] if k else gx[:, 0:BLK], y[:, k, :],
                               ACT.Square).then_inc(s.post.squared.sem, 1)
            s.post.root(act, env, ps, 0, rc)
            act.wait_ge(s.post.spread_out.sem, s.post.spread_out.d.next(act))
            act.activation(gx[:, 0:BLK], ps[:, 1:3, :].rearrange("p a b -> p (a b)"), ACT.Copy).then_inc(s.r_out.sem, 1)
            for i in range(BLK // P):
                act.wait_ge(s.o_turned.sem, s.o_turned.d.next(act))
                act.activation(ostage(i), ps[:, i, :], ACT.Copy).then_inc(s.o_out[0].sem, 1)
                if i % 2 == 1:
                    act.wait_ge(s.o_out[0].sem, s.o_out[0].d.next(act, 2))
                    store(act, i // 2)
            for i in range(BLK // P, 2 * BLK // P, 2):
                if i == 12:
                    act.wait_ge(s.o_stored[0].sem, s.o_stored[0].d.next(act, 32))
                act.wait_ge(s.o_turned.sem, s.o_turned.d.next(act, 2))
                act.activation(ostage(i + 1), ps[:, i + 1 - 8, :], ACT.Copy).then_inc(s.o_out[0].sem, 1)
                for x in s.o_out:
                    act.wait_ge(x.sem, x.d.next(act))
                store(act, i // 2)
            for x in s.o_stored:
                act.wait_ge(x.sem, x.d.next(act, 32))

        @block.vector
        def _(dve):
            hl.vector(dve, b, rbuf, raw, hhi, hlo, lambda: ring.rest(dve, G))
            for x in (A, DN):
                ring.rest(dve, x)

            def g_part():
                dve.wait_ge(s.taps.sem, s.taps.d.next(dve))
                for c in range(2):
                    dve.wait_ge(s.g_out.sem, s.g_out.d.next(dve, 3))
                    dve.wait_ge(s.conv_step.sem, s.conv_step.d.next(dve, 3))
                    dve.scalar_tensor_tensor(out=cv[c][:], in0=gx[:, 1:1 + BLK], scalar=taps[:, 1, c:c + 1],
                                             in1=cv[c][:], op0=ALU.mult, op1=ALU.add).then_inc(s.conv_step.sem, 1)
                    dve.wait_ge(s.conv_step.sem, s.conv_step.d.next(dve))
                    dve.scalar_tensor_tensor(out=cv[c][:], in0=gx[:, 2:2 + BLK], scalar=taps[:, 2, c:c + 1],
                                             in1=cv[c][:], op0=ALU.mult, op1=ALU.add).then_inc(s.conv_done.sem, 1)

            def d_part(more_g, more_d):
                for j in range(KD):
                    for t in range(2):
                        dve.wait_ge(s.d_done.sem, s.d_done.d.next(dve))
                        o = y[:, j, t * NT:(t + 1) * NT]
                        dve.tensor_tensor(o, ps[:, 5 + (2 * j + t) % 3, :], o, ALU.add).then_inc(s.d_out.sem, 1)
                    if more_g and j == 3:
                        ring.rest(dve, G)
                if more_d:
                    ring.rest(dve, DN)

            def a_part(more):
                for c in range(2):
                    dve.wait_ge(s.gelu_done.sem, s.gelu_done.d.next(dve))
                    for t in range(2):
                        dve.wait_ge(s.a_done.sem, s.a_done.d.next(dve))
                        o = cv[c][:, t * NT:(t + 1) * NT]
                        dve.tensor_tensor(o, ps[:, 3 + t, :], o, ALU.mult).then_inc(s.a_out.sem, 1)
                    dve.wait_ge(s.m_rounded.sem, s.m_rounded.d.next(dve))
                    dve.tensor_tensor(mlo[:, c, :], cv[c][:], mhi[:, c, :].bitcast(F32), ALU.subtract).then_inc(s.m_ready.sem, 1)
                if more:
                    ring.rest(dve, A)

            g_part()
            ring.rest(dve, G)
            a_part(True)
            dve.wait_ge(s.cleared.sem, s.cleared.d.next(dve))
            with repeat(dve, FG - 2, {
                    s.taps.d: 1, s.g_out.d: 6, s.conv_step.d: 8, s.d_done.d: 16, s.gelu_done.d: 2,
                    s.a_done.d: 4, s.m_rounded.d: 2, **ring.per((1, 1, 1), "rest")}):
                g_part()
                d_part(True, True)
                a_part(True)
            g_part()
            d_part(False, True)
            a_part(False)
            d_part(False, False)
            s.post.inverse(dve, rc)
            dve.wait_ge(s.r_out.sem, s.r_out.d.next(dve))
            for k in range(KD):
                dve.wait_ge(s.x_in[k % 2].sem, s.x_in[k % 2].d.next(dve, 16))
                dve.scalar_tensor_tensor(out=y[:, k, :], in0=y[:, k, :], scalar=env.gate2[:, k:k + 1],
                                         in1=gx[:, 0:BLK], op0=ALU.mult, op1=ALU.mult).then_inc(s.y_scaled.sem, 1)
                dve.wait_ge(s.y_scaled.sem, s.y_scaled.d.next(dve))
                dve.tensor_tensor(y[:, k, :], y[:, k, :], cv[k % 2][:], ALU.add).then_inc(s.x_sum.sem, 1)
            s.o_turned.d.skip(dve, BLK // P)
            for i in range(BLK // P, 2 * BLK // P, 2):
                if i == 12:
                    dve.wait_ge(s.o_stored[0].sem, s.o_stored[0].d.next(dve, 32))
                dve.wait_ge(s.o_turned.sem, s.o_turned.d.next(dve, 1 if i == BLK // P else 2))
                dve.tensor_copy(ostage(i), ps[:, i - 8, :]).then_inc(s.o_out[1].sem, 1)
            s.o_turned.d.skip(dve, 1)
            for n, x in enumerate(s.o_stored):
                x.d.skip(dve, 32)

        @block.tensor
        def _(pe):
            chunk_wait = hl.chunk_wait(pe, b)

            def up_tiles(x, done, free, bank, tiles, a0, cols):
                pe.wait_ge(ring.ready[x].sem, ring.ready[x].d.next(pe))
                for c in range(2):
                    for t in range(tiles):
                        pe.wait_ge(free.sem, free.f.next(pe))
                        a = slice(a0 + t * cols, a0 + (t + 1) * cols)
                        product(pe, ps[:, bank + t, 0:cols],
                                lambda k: (ring.hi[x][:, k * SC + c * P:k * SC + (c + 1) * P],
                                           ring.lo[x][:, k * SC + c * P:k * SC + (c + 1) * P]),
                                lambda k: (hhi[:, k, a], hlo[:, k, a]),
                                KD).then_inc(done.sem, 1)

            def first_tile(c, t):
                a = slice(t * HT, (t + 1) * HT)
                return (ps[:, 5 * c + t, 0:HT],
                        lambda k: (ring.hi[G][:, k * SC + c * P:k * SC + (c + 1) * P],
                                   ring.lo[G][:, k * SC + c * P:k * SC + (c + 1) * P]),
                        lambda k: (hhi[:, k, a], hlo[:, k, a]), s.g_done)

            def g_part():
                up_tiles(G, s.g_done, s.g_out, 0, 3, 0, HT)

            def a_part():
                up_tiles(A, s.a_done, s.a_out, 3, 2, 1, NT)

            def d_part():
                pe.wait_ge(ring.ready[DN].sem, ring.ready[DN].d.next(pe))
                pe.wait_ge(s.m_ready.sem, s.m_ready.d.next(pe, 2))
                for j in range(KD):
                    for t in range(2):
                        pe.wait_ge(s.d_out.sem, s.d_out.f.next(pe))
                        product(pe, ps[:, 5 + (2 * j + t) % 3, :],
                                lambda k: (ring.hi[DN][:, k * D + j * P:k * D + (j + 1) * P],
                                           ring.lo[DN][:, k * D + j * P:k * D + (j + 1) * P]),
                                lambda k: (mhi[:, k, t * NT:(t + 1) * NT], mlo[:, k, t * NT:(t + 1) * NT]),
                                2).then_inc(s.d_done.sem, 1)

            pe.wait_ge(ring.ready[G].sem, ring.ready[G].d.next(pe))
            s.g_out.f.skip(pe, 6)
            products_together(pe, [first_tile(c, t) for c in range(2) for t in range(3)], KD, chunk_wait)
            a_part()
            with repeat(pe, FG - 1, {
                    s.g_out.f: 6, s.a_out.f: 4, s.m_ready.d: 2, s.d_out.f: 16, **ring.per((1, 1, 1), "use")}):
                g_part()
                d_part()
                a_part()
            d_part()
            pe.wait_ge(s.g_out.sem, s.g_out.drained(pe))
            s.post.sums(pe, env, ps, 0, gx)
            s.post.spread(pe, env, ps, (1, 2), rc)
            pe.wait_ge(s.r_out.sem, s.r_out.d.next(pe))
            pe.wait_ge(s.d_out.sem, s.d_out.drained(pe))
            for k in range(KD):
                pe.wait_ge(s.x_sum.sem, s.x_sum.d.next(pe))
                if k == 4:
                    pe.wait_ge(s.o_out[0].sem, s.o_out[0].d.next(pe, BLK // P))
                for t in range(BLK // P):
                    last = pe.transpose(ps[:, t, (k % 4) * P:(k % 4 + 1) * P], y[:, k, t * P:(t + 1) * P], env.ident[:])
                    if k % 4 == 3:
                        last.then_inc(s.o_turned.sem, 1)
            s.o_out[0].d.skip(pe, 4)


def build(nc, io, out):
    env = Env()
    env.nc = nc
    env.credits, env.signals = [], []
    with ExitStack() as stack:
        env.stack = stack
        dram = lambda n, s: nc.dram_tensor(n, s, F32).ap()
        env.xt_d = dram("xt_d", [D, NTOK])
        env.r_d = dram("r_d", [NTOK])
        env.qk_d = dram("qk_d", [2 * ATT_W, NTOK])
        env.v_d = dram("v_d", [NTOK, ATT_W])
        env.ga_d = dram("ga_d", [D, SEQ])
        env.cb_d = dram("cb_d", [D, SEQ])
        env.att_d = dram("att_d", [SEQ, ATT_W])
        env.x1_d = dram("x1_d", [D, SEQ])
        env.r2_d = dram("r2_d", [SEQ])
        env.pad_d = dram("pad_d", [HEADS, 17, P])
        env.bt_d = dram("bt_d", [HEADS, P, TCOLS])
        sb = lambda n, s: stack.enter_context(nc.sbuf_tensor(n, s, F32))
        env.ident, env.ones, env.eps = sb("ident", [P, P]), sb("ones", [P, P]), sb("eps", [P, 1])
        env.param, env.csil = sb("param", [P, 196]), sb("csil", [P, 16])
        env.shift1, env.scale1, env.gate1 = sb("shift1", [P, KD]), sb("scale1", [P, KD]), sb("gate1", [P, KD])
        env.shift2, env.scale2, env.gate2 = sb("shift2", [P, KD]), sb("scale2", [P, KD]), sb("gate2", [P, KD])
        env.shiftc, env.scalec = sb("shiftc", [P, KD]), sb("scalec", [P, KD])
        env.ring, env.hload = Ring(env), HLoad(env)
        env.psig = make_projection_signals(env)
        env.pad_dma = Signal(env, "pad_dma")
        env.tab_in = [Signal(env, f"tab_in{i}") for i in range(2)]
        env.tab_stored = [Signal(env, f"tab_stored{i}") for i in range(2)]
        with ExitStack() as own:
            env.stack, env.signals = own, []
            setup(nc, env, io)
            with nc.Block() as block:
                @block.gpsimd
                def _(pool):
                    for s in env.signals:
                        pool.sem_clear(s.sem)
        env.stack = stack
        env.asig = make_attention_signals(env)
        env.msig, env.fsig = make_merge_signals(env), make_ffn_signals(env)
        with nc.Block() as block:
            @block.gpsimd
            def _(pool):
                for s in env.credits:
                    pool.sem_inc(s.sem, s.credit)
        for b in (None, 0, 1):
            projections(nc, env, io, b)
        attention(nc, env, io)
        for b in range(NB):
            merge(nc, env, io, b)
        for b in range(NB):
            ffn(nc, env, io, out, b)


_INS = ["x", "c", "ctx", "c_ctx", "w_ada", "b_ada", "g_pre_mix", "g_post_mix", "g_pre_ffn", "g_post_ffn",
        "w_in", "rpb", "w_short_conv", "w_branch_attn", "w_branch_conv", "w_out",
        "w_up", "w_ffn_conv", "b_ffn_conv", "w_down"]


def kernel(**inputs):
    import concourse.bacc as bacc
    from concourse.bass_utils import run_bass_kernel_spmd

    nc = bacc.Bacc("TRN2", target_bir_lowering=False, num_devices=1)
    arrays, io = {}, {}
    for name in _INS:
        a = np.ascontiguousarray(inputs[name])
        arrays[f"in_{name}"] = a
        io[name] = nc.dram_tensor(f"in_{name}", a.shape, mybir.dt.from_np(a.dtype), kind="ExternalInput").ap()
    out = nc.dram_tensor("out_0", (1, SEQ, D), F32, kind="ExternalOutput").ap()
    build(nc, io, out)
    r = run_bass_kernel_spmd(nc, [arrays], core_ids=[0])
    return r.results[0]["out_0"]
```
